# Optimizing a Trainium2 kernel written in Bass

```python
import jax
import jax.numpy as jnp
from jax import lax
import numpy as np

D_MODEL = 2048
BATCH = 1
SEQ = 256
DEPTH = 2

MIX_WIDTH = D_MODEL
D_A = MIX_WIDTH // 2
D_B = MIX_WIDTH // 2
D_C = MIX_WIDTH // 2
D_D = MIX_WIDTH // 2
POOL_WINDOWS = (2, 4, 8, 16)
POOL_GROUPS = len(POOL_WINDOWS)
POOL_GC = D_A // POOL_GROUPS
SHORT_CONV = 3
SGU_CHUNK = 128
SGU_HEADS = 8
SGU_HD = D_C // SGU_HEADS
CONF_KERNEL = 31
CONF_GROUPS = 8
CONF_GD = D_D // CONF_GROUPS
PEER_HEADS = 8
PEER_NKEYS = 128
PEER_EXPERTS = PEER_NKEYS * PEER_NKEYS
PEER_TOPK = 16
PEER_DK = 128
PEER_DKH = PEER_DK // 2
PEER_TOKEN_CHUNK = 128
EPS = 1e-6

kernel_name = 'hybrid_pool_shortconv_sgu_conformer_peer'

def rms_norm(x, g):
    x32 = x.astype(jnp.float32)
    y = x32 * lax.rsqrt(jnp.mean(x32 * x32, axis=-1, keepdims=True) + EPS)
    return (y * g).astype(x.dtype)

def layer_norm(x, g, b):
    x32 = x.astype(jnp.float32)
    mu = jnp.mean(x32, axis=-1, keepdims=True)
    xc = x32 - mu
    y = xc * lax.rsqrt(jnp.mean(xc * xc, axis=-1, keepdims=True) + EPS)
    return (y * g + b).astype(x.dtype)

def causal_dwconv(x, w):
    k, c = w.shape
    return lax.conv_general_dilated(
        x, w[:, None, :], window_strides=(1,), padding=((k - 1, 0),),
        dimension_numbers=('NWC', 'WIO', 'NWC'), feature_group_count=c)

def pool_mixer(xa, w, scale):
    bsz, s, _ = xa.shape
    xg = xa.astype(jnp.float32).reshape(bsz, s, POOL_GROUPS, POOL_GC)
    csum = jnp.cumsum(xg, axis=1)
    pos = jnp.arange(s, dtype=jnp.int32)
    outs = []
    for g, win in enumerate(POOL_WINDOWS):
        c = csum[:, :, g]
        lag = jnp.pad(c, ((0, 0), (win, 0), (0, 0)))[:, :s]
        cnt = jnp.minimum(pos + 1, win).astype(jnp.float32)[None, :, None]
        outs.append((c - lag) / cnt - xg[:, :, g])
    pooled = jnp.stack(outs, axis=2).astype(xa.dtype)
    mixed = jnp.einsum('bsgc,gcd->bsgd', pooled, w).reshape(bsz, s, D_A)
    return mixed * scale

def spatial_gating(u, v, ln_g, ln_b, ws, bs):
    u = jax.nn.gelu(u, approximate=False)
    v = layer_norm(jax.nn.gelu(v, approximate=False), ln_g, ln_b)
    bsz, s, _ = v.shape
    vh = v.reshape(bsz, s // SGU_CHUNK, SGU_CHUNK, SGU_HEADS, SGU_HD)
    mask = jnp.tril(jnp.ones((SGU_CHUNK, SGU_CHUNK), dtype=bool))
    wm = jnp.where(mask[None], ws, jnp.zeros((), ws.dtype))
    mixed = jnp.einsum('hts,bnshc->bnthc', wm, vh) + jnp.transpose(bs)[None, None, :, :, None]
    return u * mixed.reshape(bsz, s, D_C)

def conformer_conv(a, g, conv_w, conv_b, gn_g, gn_b):
    z = a * jax.nn.sigmoid(g)
    z = causal_dwconv(z, conv_w) + conv_b
    bsz, s, _ = z.shape
    z32 = z.astype(jnp.float32).reshape(bsz, s, CONF_GROUPS, CONF_GD)
    mu = jnp.mean(z32, axis=-1, keepdims=True)
    zc = z32 - mu
    zn = (zc * lax.rsqrt(jnp.mean(zc * zc, axis=-1, keepdims=True) + EPS)).reshape(bsz, s, D_D)
    zn = (zn * gn_g + gn_b).astype(z.dtype)
    return jax.nn.silu(zn)

def peer_ffn(xn, w_q, subkeys, u_tab, v_tab):
    bsz, s, d = xn.shape
    t = bsz * s
    xt = xn.reshape(t, d)
    q = (xt @ w_q).reshape(t, PEER_HEADS, 2, PEER_DKH)
    scores = jnp.einsum('thpk,hpnk->thpn', q.astype(jnp.float32), subkeys.astype(jnp.float32))
    s_top, i_top = lax.top_k(scores, PEER_TOPK)
    cand_s = s_top[:, :, 0, :, None] + s_top[:, :, 1, None, :]
    cand_i = i_top[:, :, 0, :, None] * PEER_NKEYS + i_top[:, :, 1, None, :]
    kk = PEER_TOPK * PEER_TOPK
    f_s, f_pos = lax.top_k(cand_s.reshape(t, PEER_HEADS, kk), PEER_TOPK)
    e_idx = jnp.take_along_axis(cand_i.reshape(t, PEER_HEADS, kk), f_pos, axis=-1)
    gates = jax.nn.softmax(f_s, axis=-1).astype(xn.dtype)
    n_sel = PEER_HEADS * PEER_TOPK
    n_blk = t // PEER_TOKEN_CHUNK

    def block_fn(args):
        xc, ic, gc = args
        uc = jnp.take(u_tab, ic, axis=0)
        act = gc * jax.nn.gelu(jnp.einsum('cd,ced->ce', xc, uc), approximate=False)
        vc = jnp.take(v_tab, ic, axis=0)
        return jnp.einsum('ce,ced->cd', act, vc)

    out = lax.map(block_fn, (xt.reshape(n_blk, PEER_TOKEN_CHUNK, d),
                             e_idx.reshape(n_blk, PEER_TOKEN_CHUNK, n_sel),
                             gates.reshape(n_blk, PEER_TOKEN_CHUNK, n_sel)))
    return out.reshape(bsz, s, d)

def setup_inputs(seed: int = 0) -> dict:
    key = jax.random.key(seed)
    ks = jax.random.split(key, 24)
    n_ev = (DEPTH + 1) // 2
    n_od = DEPTH // 2

    def nrm(k, shape, scale):
        return jax.random.normal(k, shape, jnp.float32) * scale

    return {
        'x': nrm(ks[0], (BATCH, SEQ, D_MODEL), 1.0),
        'mix_norm_g': 1.0 + nrm(ks[1], (DEPTH, D_MODEL), 0.1),
        'ffn_norm_g': 1.0 + nrm(ks[2], (DEPTH, D_MODEL), 0.1),
        'ev_w_in': nrm(ks[3], (n_ev, D_MODEL, D_A + 3 * D_B), D_MODEL ** -0.5),
        'ev_pool_w': nrm(ks[4], (n_ev, POOL_GROUPS, POOL_GC, POOL_GC), POOL_GC ** -0.5),
        'ev_pool_scale': 1.0 + nrm(ks[5], (n_ev, D_A), 0.1),
        'ev_conv_w': nrm(ks[6], (n_ev, SHORT_CONV, D_B), SHORT_CONV ** -0.5),
        'ev_w_out': nrm(ks[7], (n_ev, D_A + D_B, D_MODEL), (D_A + D_B) ** -0.5),
        'od_w_in': nrm(ks[8], (n_od, D_MODEL, 2 * D_C + 2 * D_D), D_MODEL ** -0.5),
        'od_v_norm_g': 1.0 + nrm(ks[9], (n_od, D_C), 0.1),
        'od_v_norm_b': nrm(ks[10], (n_od, D_C), 0.02),
        'od_sgu_w': nrm(ks[11], (n_od, SGU_HEADS, SGU_CHUNK, SGU_CHUNK), SGU_CHUNK ** -0.5),
        'od_sgu_b': 1.0 + nrm(ks[12], (n_od, SGU_HEADS, SGU_CHUNK), 0.1),
        'od_conv_w': nrm(ks[13], (n_od, CONF_KERNEL, D_D), CONF_KERNEL ** -0.5),
        'od_conv_b': nrm(ks[14], (n_od, D_D), 0.02),
        'od_gn_g': 1.0 + nrm(ks[15], (n_od, D_D), 0.1),
        'od_gn_b': nrm(ks[16], (n_od, D_D), 0.02),
        'od_w_out': nrm(ks[17], (n_od, D_C + D_D, D_MODEL), (D_C + D_D) ** -0.5),
        'peer_w_q': nrm(ks[18], (DEPTH, D_MODEL, PEER_HEADS * PEER_DK), D_MODEL ** -0.5),
        'peer_subkeys': nrm(ks[19], (DEPTH, PEER_HEADS, 2, PEER_NKEYS, PEER_DKH), PEER_DKH ** -0.5),
        'peer_u': nrm(ks[20], (DEPTH, PEER_EXPERTS, D_MODEL), D_MODEL ** -0.5),
        'peer_v': nrm(ks[21], (DEPTH, PEER_EXPERTS, D_MODEL), PEER_HEADS ** -0.5),
        'final_norm_g': 1.0 + nrm(ks[22], (D_MODEL,), 0.1),
    }

def reference(x, mix_norm_g, ffn_norm_g, ev_w_in, ev_pool_w, ev_pool_scale, ev_conv_w, ev_w_out,
              od_w_in, od_v_norm_g, od_v_norm_b, od_sgu_w, od_sgu_b, od_conv_w, od_conv_b,
              od_gn_g, od_gn_b, od_w_out, peer_w_q, peer_subkeys, peer_u, peer_v, final_norm_g):
    h = x
    for layer in range(DEPTH):
        j = layer // 2
        z = rms_norm(h, mix_norm_g[layer])
        if layer % 2 == 0:
            p = z @ ev_w_in[j]
            xa, bg, cg, hb = jnp.split(p, [D_A, D_A + D_B, D_A + 2 * D_B], axis=-1)
            ya = pool_mixer(xa, ev_pool_w[j], ev_pool_scale[j])
            yb = bg * causal_dwconv(cg * hb, ev_conv_w[j])
            mix = jnp.concatenate([ya, yb], axis=-1) @ ev_w_out[j]
        else:
            p = z @ od_w_in[j]
            u, v, a, g = jnp.split(p, [D_C, 2 * D_C, 2 * D_C + D_D], axis=-1)
            yc = spatial_gating(u, v, od_v_norm_g[j], od_v_norm_b[j], od_sgu_w[j], od_sgu_b[j])
            yd = conformer_conv(a, g, od_conv_w[j], od_conv_b[j], od_gn_g[j], od_gn_b[j])
            mix = jnp.concatenate([yc, yd], axis=-1) @ od_w_out[j]
        h = h + mix
        h = h + peer_ffn(rms_norm(h, ffn_norm_g[layer]), peer_w_q[layer], peer_subkeys[layer],
                         peer_u[layer], peer_v[layer])
    return rms_norm(h, final_norm_g)


_drawn_inputs = setup_inputs


def setup_inputs(seed=0):
    import zlib

    import numpy as np

    out = dict(_drawn_inputs(seed))
    spreads = {}
    factors = {'od_v_norm_b': 6.881, 'od_conv_b': 3.213, 'od_gn_b': 5.153}
    for name, (base, spread) in spreads.items():
        noise = np.random.default_rng([zlib.crc32(name.encode()), seed]).standard_normal(out[name].shape)
        drawn = base * np.exp(spread * noise) if base else spread * noise
        out[name] = jnp.asarray(drawn.astype(out[name].dtype))
    for name, factor in factors.items():
        out[name] = (out[name] * factor).astype(out[name].dtype)
    return out
```

```python
from contextlib import ExitStack

import concourse.bass as bass
from concourse import mybir

F32 = mybir.dt.float32
I32 = mybir.dt.int32
U32 = mybir.dt.uint32
ALU = mybir.AluOpType
ACT = mybir.ActivationFunctionType
AX = mybir.AxisListType

P = 128
D = 2048
SEQ = 256
BLOCKS = SEQ // P
KD = D // P
LAYERS = 2
BANK = 512
WCOLS = 256
WSLOTS = 4
SECTION = WSLOTS * WCOLS
CH = SECTION // P
IN_TILES = 4 * WSLOTS
OUT_TILES = KD // 2
Q_TILES = WSLOTS
TILES = IN_TILES + OUT_TILES + Q_TILES
WINDOWS = (2, 4, 8, 16)
SHORT = 3
TAPS = 31
HEADS = 8
TOPK = 16
NKEYS = 128
SEL = 2 * NKEYS
USLOTS, VSLOTS = 4, 8
EPS = 1e-6
LOWEST = -3.0e38

ROWS_MIX, ROWS_FFN, ROWS_SCALE, ROWS_SHORT = 0, 32, 64, 72
ROWS_CONVB, ROWS_GNG, ROWS_GNB, ROWS_A = 96, 104, 112, 120
ROWS_B = TAPS * CH // 2


def two_layers(nc, x, mix_norm_g, ffn_norm_g, ev_w_in, ev_pool_w, ev_pool_scale, ev_conv_w, ev_w_out,
               od_w_in, od_v_norm_g, od_v_norm_b, od_sgu_w, od_sgu_b, od_conv_w, od_conv_b,
               od_gn_g, od_gn_b, od_w_out, peer_w_q, peer_subkeys, peer_u, peer_v, final_norm_g, out):
    w_in = (ev_w_in[0], od_w_in[0])
    w_out = (ev_w_out[0], od_w_out[0])
    by_rows = lambda w: w.rearrange("(k p) c -> p k c", p=P)
    chunked = lambda v: v.rearrange("(r c) -> r c", c=P)

    with ExitStack() as ctx:
        sb = lambda name, shape, dt=F32: ctx.enter_context(nc.sbuf_tensor(name, shape, dt))
        sem = lambda name: ctx.enter_context(nc.semaphore(name))

        h = sb("h", [P, BLOCKS, D])
        zn = sb("zn", [P, BLOCKS, D])
        yT = zn[:, :, :].rearrange("p b (k t) -> p (b k) t", t=SEQ)
        zT = sb("zT", [P, KD, SEQ])
        scores = zT[:, :, :].rearrange("p (b h) n -> p b h n", b=BLOCKS)
        WSIZE = KD * WCOLS
        arena = sb("arena", [P, WSLOTS * WSIZE + 32 * SEQ])
        wslot = [arena[:, s * WSIZE:(s + 1) * WSIZE].rearrange("p (k c) -> p k c", c=WCOLS) for s in range(WSLOTS)]
        oslot = [arena[:, s * WSIZE:(s + 1) * WSIZE].rearrange("p (k c) -> p k c", c=D) for s in range(WSLOTS)]
        proj_at = WSLOTS * WSIZE
        proj = arena[:, proj_at:proj_at + 32 * SEQ].rearrange("p (k t) -> p k t", t=SEQ)
        vt = arena[:, proj_at + 24 * SEQ:proj_at + 32 * SEQ].rearrange("p (b c) -> p b c", b=BLOCKS)
        qT = proj[:, 0:CH, :]
        uslot = [arena[:, s * D:(s + 1) * D] for s in range(USLOTS)]
        vslot = [arena[:, (USLOTS + s) * D:(USLOTS + s + 1) * D] for s in range(VSLOTS)]
        gB = sb("gB", [P, D])
        shared = sb("shared", [P, 2 * SECTION])
        poolw = shared[:, :].rearrange("p (k d) -> p k d", d=WCOLS)
        vgb = shared[:, :].rearrange("p (a c) -> p a c", a=2)
        subraw = sb("subraw", [P, HEADS, P])
        subT = sb("subT", [P, HEADS, SEL])
        sguraw = sb("sguraw", [P, HEADS, P])
        wmT = sb("wmT", [P, HEADS, P])
        sgub = sb("sgub", [1, HEADS * P])
        scratch = sb("scratch", [P, CH * (SEQ + TAPS - 1)])
        padded = scratch[:, :].rearrange("p (c t) -> p c t", c=CH)
        SP_ = SEQ + SHORT - 1
        padshort = scratch[:, 0:CH * SP_].rearrange("p (c t) -> p c t", c=CH)
        WP = SEQ + WINDOWS[-1]
        padpool = scratch[:, 0:4 * WP].rearrange("p (a c t) -> p a c t", a=2, c=2)
        diag = scratch[:, 0:TOPK * P].rearrange("p (j c) -> p j c", c=P)
        ident = sb("ident", [P, P])
        mean_of = sb("mean_of", [P, P])
        ones_row = sb("ones_row", [1, P])
        zeros = sb("zeros", [P, P], mybir.dt.bfloat16)
        eps_col = sb("eps_col", [P, 1])
        paramrow = sb("paramrow", [P, 3, P])
        colA = sb("colA", [P, ROWS_A])
        convT = sb("convT", [P, TAPS * CH])
        inv_count = sb("inv_count", [P, SEQ])
        position = sb("position", [P, SEQ])
        iota16 = sb("iota16", [P, TOPK])
        square_sum = sb("square_sum", [P, BLOCKS])
        root = sb("root", [P, BLOCKS])
        rstd = sb("rstd", [P, BLOCKS])
        vsum = sb("vsum", [P, BLOCKS, WSLOTS])
        vstat = sb("vstat", [P, 4, BLOCKS])
        sc = sb("sc", [P, 2, NKEYS])
        sc2 = sb("sc2", [P, 2, NKEYS])
        top = sb("top", [P, 2, TOPK])
        topi = sb("topi", [P, 2, TOPK], U32)
        topf = sb("topf", [P, 2, TOPK])
        cand = sb("cand", [P, TOPK, TOPK])
        cand2 = sb("cand2", [P, TOPK * TOPK])
        best = sb("best", [P, TOPK])
        besti = sb("besti", [P, TOPK], U32)
        pos = sb("pos", [P, 2, TOPK], U32)
        onehot = sb("onehot", [P, 2, TOPK, TOPK])
        key = sb("key", [P, 2, TOPK])
        below = sb("below", [P, TOPK])
        expo = sb("expo", [P, TOPK])
        denom = sb("denom", [P, 2])
        gates = sb("gates", [P, TOPK])
        expert_u = sb("expert_u", [P, TOPK], I32)
        expert_v = sb("expert_v", [P, TOPK], I32)
        dots = sb("dots", [P, TOPK])
        gelu = sb("gelu", [P, TOPK])
        weight = sb("weight", [P, TOPK])
        token = sb("token", [P, 2 + 2 * LAYERS])
        ps = ctx.enter_context(nc.psum_tensor("ps", [P, 8, BANK], F32))

        made = sem("made")
        x_in = sem("x_in")
        rows_in = sem("rows_in")
        gain_in = sem("gain_in")
        shared_in = sem("shared_in")
        keys_in = sem("keys_in")
        sgu_in = sem("sgu_in")
        w_in_slot = [sem(f"w_in_slot{s}") for s in range(WSLOTS)]
        w_free = sem("w_free")
        squared = sem("squared")
        rooted = sem("rooted")
        rstd_ready = sem("rstd_ready")
        zn_ready = sem("zn_ready")
        turned = sem("turned")
        zT_even = sem("zT_even")
        zT_odd = sem("zT_odd")
        xn_ready = sem("xn_ready")
        params_turned = sem("params_turned")
        cols_ready = sem("cols_ready")
        keys_turned = sem("keys_turned")
        keys_ready = sem("keys_ready")
        sgu_turned = sem("sgu_turned")
        sgu_copied = sem("sgu_copied")
        sgu_ready = sem("sgu_ready")
        tile_out = sem("tile_out")
        pooled = sem("pooled")
        pool_mixed = sem("pool_mixed")
        pool_out = sem("pool_out")
        conv_out = sem("conv_out")
        conv_step = sem("conv_step")
        v_squared = sem("v_squared")
        v_centred = sem("v_centred")
        v_root = sem("v_root")
        v_ready = sem("v_ready")
        gn_mean = sem("gn_mean")
        gn_centred = sem("gn_centred")
        gn_squared = sem("gn_squared")
        gn_var = sem("gn_var")
        gn_root = sem("gn_root")
        gn_scaled = sem("gn_scaled")
        gn_out = sem("gn_out")
        gated = sem("gated")
        sgu_out = sem("sgu_out")
        h_mixed = sem("h_mixed")
        q_scored = sem("q_scored")
        scores_out = sem("scores_out")
        head_in = sem("head_in")
        under_max = sem("under_max")
        exp_done = sem("exp_done")
        experts_u = sem("experts_u")
        experts_v = sem("experts_v")
        u_in = [sem(f"u_in{s}") for s in range(USLOTS)]
        v_in = [sem(f"v_in{s}") for s in range(VSLOTS)]
        u_free = sem("u_free")
        v_free = sem("v_free")
        gelu_done = sem("gelu_done")
        weights_done = sem("weights_done")
        diag_done = sem("diag_done")
        block_done = sem("block_done")
        h_expert = sem("h_expert")
        result_ready = sem("result_ready")
        stored = sem("stored")
        dve_step = sem("dve_step")
        route_step = sem("route_step")

        SLOTS_FREED_U = USLOTS + BLOCKS * HEADS * TOPK
        SLOTS_FREED_V = VSLOTS + BLOCKS * HEADS * TOPK
        CONSTANTS = 9

        block = ctx.enter_context(nc.Block())

        def wait_unfused(eng, *waits):
            for _, value in waits:
                eng.to_reg(value)
            eng.wait_ge(made, CONSTANTS)
            for s, value in waits:
                eng.wait_ge(s, value)

        @block.sync
        def _(sp):
            for b in range(BLOCKS):
                sp.dma_start(h[:, b, :], x[0, b * P:(b + 1) * P, :]).then_inc(x_in, 16)
            rows = paramrow
            sp.dma_start(rows[ROWS_MIX:ROWS_MIX + 32, 0, :],
                         mix_norm_g.rearrange("l (k c) -> (l k) c", c=P)).then_inc(rows_in, 16)
            sp.dma_start(rows[ROWS_FFN:ROWS_FFN + 32, 0, :],
                         ffn_norm_g.rearrange("l (k c) -> (l k) c", c=P)).then_inc(rows_in, 16)
            sp.dma_start(rows[ROWS_SCALE:ROWS_SCALE + CH, 0, :], chunked(ev_pool_scale[0])).then_inc(rows_in, 16)
            sp.dma_start(rows[ROWS_SHORT:ROWS_SHORT + SHORT * CH, 0, :],
                         ev_conv_w[0].rearrange("k (r c) -> (k r) c", c=P)).then_inc(rows_in, 16)
            sp.dma_start(rows[ROWS_CONVB:ROWS_CONVB + CH, 0, :], chunked(od_conv_b[0])).then_inc(rows_in, 16)
            sp.dma_start(rows[ROWS_GNG:ROWS_GNG + CH, 0, :], chunked(od_gn_g[0])).then_inc(rows_in, 16)
            sp.dma_start(rows[ROWS_GNB:ROWS_GNB + CH, 0, :], chunked(od_gn_b[0])).then_inc(rows_in, 16)
            taps = od_conv_w[0].rearrange("k (r c) -> (k r) c", c=P)
            sp.dma_start(rows[0:ROWS_B, 1, :], taps[0:ROWS_B, :]).then_inc(rows_in, 16)
            sp.dma_start(rows[0:ROWS_B, 2, :], taps[ROWS_B:2 * ROWS_B, :]).then_inc(rows_in, 16)

            for L in range(LAYERS):
                win, wout, wq = by_rows(w_in[L]), by_rows(w_out[L]), by_rows(peer_w_q[L])
                if L:
                    sp.wait_ge(h_expert, BLOCKS * L)
                    sp.dma_start(sguraw[:, :, :], od_sgu_w[0].rearrange("h t s -> t h s")).then_inc(sgu_in, 16)
                    sp.dma_start(sgub[0:1, :], od_sgu_b[0:1].rearrange("o h t -> o (h t)")).then_inc(sgu_in, 16)
                    sp.dma_start(vgb[:, 0, :], od_v_norm_g[0:1, :].to_broadcast([P, SECTION])).then_inc(shared_in, 16)
                    sp.dma_start(vgb[:, 1, :], od_v_norm_b[0:1, :].to_broadcast([P, SECTION]))\
                      .then_inc(shared_in, 16)
                sp.dma_start(subraw[:, :, :].rearrange("n h (p k) -> n h p k", p=2),
                             peer_subkeys[L].rearrange("h p n k -> n h p k")).then_inc(keys_in, 16)
                if L == 0:
                    with sp.Fori(0, 4) as i:
                        for t in range(WSLOTS):
                            sp.wait_ge(w_free, i * WSLOTS + t + 1)
                            sp.dma_start(wslot[t], win[:, :, bass.ds(i * SECTION + t * WCOLS, WCOLS)])\
                              .then_inc(w_in_slot[t], 16)
                else:
                    for i, part in enumerate((2, 3, 1, 0)):
                        for t in range(WSLOTS):
                            sp.wait_ge(w_free, L * TILES + i * WSLOTS + t + 1)
                            at = part * SECTION + t * WCOLS
                            sp.dma_start(wslot[t], win[:, :, at:at + WCOLS]).then_inc(w_in_slot[t], 16)
                if L == 0:
                    sp.dma_start(poolw, ev_pool_w[0].rearrange("g (k p) d -> p (g k) d", p=P))\
                      .then_inc(shared_in, 16)
                sp.dma_start(gB[:, :], ffn_norm_g[L:L + 1, :].to_broadcast([P, D])).then_inc(gain_in, 16)
                with sp.Fori(0, OUT_TILES // WSLOTS) as i:
                    for t in range(WSLOTS):
                        sp.wait_ge(w_free, i * WSLOTS + (L * TILES + IN_TILES + t + 1))
                        sp.dma_start(oslot[t], wout[:, bass.ds((i * WSLOTS + t) * 2, 2), :])\
                          .then_inc(w_in_slot[t], 16)
                for t in range(WSLOTS):
                    sp.wait_ge(w_free, L * TILES + IN_TILES + OUT_TILES + t + 1)
                    sp.dma_start(wslot[t], wq[:, :, t * WCOLS:(t + 1) * WCOLS]).then_inc(w_in_slot[t], 16)
            sp.wait_ge(xn_ready, BLOCKS * LAYERS)
            sp.dma_start(gB[:, :], final_norm_g.rearrange("(a c) -> a c", a=1).to_broadcast([P, D]))\
              .then_inc(gain_in, 16)
            for b in range(BLOCKS):
                sp.wait_ge(result_ready, b + 1)
                sp.dma_start(out[0, b * P:(b + 1) * P, :], zn[:, b, :]).then_inc(stored, 16)
            sp.wait_ge(stored, 16 * BLOCKS)

        @block.gpsimd
        def _(pool):
            g = nc.gpsimd
            g.memset(ident[:, :], 0.0).then_inc(made, 1)
            g.memset(mean_of[:, :], 1.0 / P).then_inc(made, 1)
            g.memset(ones_row[:, :], 1.0).then_inc(made, 1)
            g.memset(zeros[:, :], 0.0).then_inc(made, 1)
            g.memset(eps_col[:, :], EPS).then_inc(made, 1)
            g.memset(subT[:, :, :], 0.0).then_inc(made, 1)
            g.iota(position[:, :], pattern=[[1, SEQ]], base=1, channel_multiplier=0,
                   allow_small_or_imprecise_dtypes=True).then_inc(made, 1)
            g.iota(iota16[:, :], pattern=[[1, TOPK]], base=0, channel_multiplier=0,
                   allow_small_or_imprecise_dtypes=True).then_inc(made, 1)
            pool.wait_ge(made, 1)
            g.affine_select(out=ident[:, :], in_=ident[:, :], compare_op=ALU.not_equal, fill=1.0, base=0,
                            pattern=[[-1, P]], channel_multiplier=1).then_inc(made, 1)

            def experts(L):
                for b in range(BLOCKS):
                    heads = (L * BLOCKS + b) * HEADS
                    ufreed = L * SLOTS_FREED_U + b * HEADS * TOPK
                    vfreed = L * SLOTS_FREED_V + b * HEADS * TOPK
                    with pool.Fori(0, HEADS) as i:
                        for j in range(TOPK):
                            listed = [(experts_u, i + (heads + 1))] if j == 0 else []
                            wait_unfused(pool, *listed, (u_free, i * TOPK + (ufreed + j + 1)))
                            g.indirect_dma_start(
                                out=uslot[j % USLOTS], out_offset=None, in_=peer_u.rearrange("l e d -> (l e) d"),
                                in_offset=bass.IndirectOffsetOnAxis(ap=expert_u[:, j:j + 1], axis=0),
                            ).then_inc(u_in[j % USLOTS], 16)
                        for j in range(TOPK):
                            listed = [(experts_v, i + (heads + 1))] if j == 0 else []
                            wait_unfused(pool, *listed, (v_free, i * TOPK + (vfreed + j + 1)))
                            g.indirect_dma_start(
                                out=vslot[j % VSLOTS], out_offset=None, in_=peer_v.rearrange("l e d -> (l e) d"),
                                in_offset=bass.IndirectOffsetOnAxis(ap=expert_v[:, j:j + 1], axis=0),
                            ).then_inc(v_in[j % VSLOTS], 16)

            experts(0)
            pool.wait_ge(sgu_copied, 2)
            g.affine_select(out=wmT[:, :, :], in_=wmT[:, :, :], compare_op=ALU.is_ge, fill=0.0, base=0,
                            pattern=[[0, HEADS], [1, P]], channel_multiplier=-1).then_inc(sgu_ready, 1)
            experts(1)

        @block.tensor
        def _(pe):
            mm = nc.tensor.matmul

            def transposes(m):
                pe.wait_ge(zn_ready, BLOCKS * (m + 1))
                for kk in range(KD // 2):
                    if kk >= 4:
                        pe.wait_ge((zT_even, zT_odd)[kk % 2], (KD // 2) * m + 2 * ((kk - 4) // 2 + 1))
                    for k in (2 * kk, 2 * kk + 1):
                        for b in range(BLOCKS):
                            at = (k % 2) * SEQ + b * P
                            last = nc.tensor.transpose(ps[:, kk % 4, at:at + P], zn[:, b, k * P:(k + 1) * P],
                                                       ident[:, :])
                    last.then_inc(turned, 1)
                pe.wait_ge(zT_even, (KD // 2) * (m + 1))
                pe.wait_ge(zT_odd, (KD // 2) * (m + 1))

            def channel_tile(t):
                for c in range(WCOLS // P):
                    for k in range(KD):
                        last = mm(ps[:, t, c * SEQ:(c + 1) * SEQ], wslot[t][:, k, c * P:(c + 1) * P], zT[:, k, :],
                                  start=(k == 0), stop=(k == KD - 1))
                return last

            def project(L, n0, bank0):
                for t in range(WSLOTS):
                    pe.wait_ge(w_in_slot[t], 16 * (L * TILES // WSLOTS + n0 // WSLOTS + 1))
                    pe.wait_ge(tile_out, bank0 + t + 1)
                    channel_tile(t).then_inc(w_free, 1)

            def project_loop(L, n0, bank0, count):
                with pe.Fori(0, count) as i:
                    for t in range(WSLOTS):
                        pe.wait_ge(w_in_slot[t], i * 16 + 16 * (L * TILES // WSLOTS + n0 // WSLOTS + 1))
                        pe.wait_ge(tile_out, i * WSLOTS + (bank0 + t + 1))
                        channel_tile(t).then_inc(w_free, 1)

            pe.wait_ge(made, CONSTANTS)
            pe.wait_ge(rows_in, 16 * 9)
            nc.tensor.transpose(ps[:, 6, 0:ROWS_A], paramrow[0:ROWS_A, 0, :], ident[0:ROWS_A, 0:ROWS_A])
            for a in range(2):
                last = nc.tensor.transpose(ps[:, 6, (a + 1) * P:(a + 1) * P + ROWS_B], paramrow[0:ROWS_B, a + 1, :],
                                           ident[0:ROWS_B, 0:ROWS_B])
            last.then_inc(params_turned, 1)

            BANKS = IN_TILES + Q_TILES
            for L in range(LAYERS):
                transposes(2 * L)
                pe.wait_ge(keys_in, 16 * (L + 1))
                for hd in range(HEADS):
                    last = nc.tensor.transpose(ps[:, 4 + hd // 4, (hd % 4) * P:(hd % 4 + 1) * P], subraw[:, hd, :],
                                               ident[:, :])
                last.then_inc(keys_turned, 1)
                if L == 0:
                    project_loop(L, 0, 0, 4)
                    pe.wait_ge(shared_in, 16)
                    pe.wait_ge(keys_ready, 2)
                    for gr in range(len(WINDOWS)):
                        pe.wait_ge(pooled, gr + 1)
                        for dd in range(2):
                            for kc in range(2):
                                last = mm(ps[:, 4 + gr, dd * SEQ:(dd + 1) * SEQ],
                                          poolw[:, 2 * gr + kc, dd * P:(dd + 1) * P], proj[:, 2 * gr + kc, :],
                                          start=(kc == 0), stop=(kc == 1))
                        last.then_inc(pool_mixed, 1)
                    pe.wait_ge(pool_out, CH)
                    pe.wait_ge(conv_out, CH)
                else:
                    pe.wait_ge(sgu_in, 32)
                    for hd in range(HEADS):
                        last = nc.tensor.transpose(ps[:, 6 + hd // 4, (hd % 4) * P:(hd % 4 + 1) * P],
                                                   sguraw[:, hd, :], ident[:, :])
                    last.then_inc(sgu_turned, 1)
                    bank0 = BANKS * L
                    project_loop(L, 0, bank0, 2)
                    for t in range(WSLOTS):
                        pe.wait_ge(w_in_slot[t], 16 * (L * TILES // WSLOTS + 3))
                        pe.wait_ge(tile_out, bank0 + 2 * WSLOTS + t + 1)
                        for b in range(BLOCKS):
                            for k in range(KD):
                                last = mm(ps[:, t, b * WCOLS:(b + 1) * WCOLS], zT[:, k, b * P:(b + 1) * P],
                                          wslot[t][:, k, :], start=(k == 0), stop=(k == KD - 1))
                        last.then_inc(w_free, 1)
                    project(L, 3 * WSLOTS, bank0 + 3 * WSLOTS)
                    pe.wait_ge(conv_step, TAPS * CH)
                    pe.wait_ge(keys_ready, 4)
                    pe.wait_ge(sgu_copied, 2)
                    for c2 in range(CH // 2):
                        mm(ps[:, 4 + c2, :], mean_of[:, :], proj[:, 2 * c2:2 * c2 + 2, :],
                           start=True, stop=True).then_inc(gn_mean, 1)
                    pe.wait_ge(v_ready, BLOCKS)
                    pe.wait_ge(sgu_ready, 1)
                    pe.wait_ge(tile_out, WSLOTS + BANKS + IN_TILES)
                    for hd in range(HEADS):
                        for b in range(BLOCKS):
                            o = ps[:, hd // 2, (hd % 2) * SEQ + b * P:(hd % 2) * SEQ + (b + 1) * P]
                            mm(o, ones_row[0:1, :], sgub[0:1, hd * P:(hd + 1) * P], start=True, stop=False)
                            last = mm(o, vt[:, b, hd * P:(hd + 1) * P], wmT[:, hd, :], start=False, stop=True)
                        if hd % 2:
                            last.then_inc(gated, 1)
                    for c2 in range(CH // 2):
                        pe.wait_ge(gn_squared, c2 + 1)
                        mm(ps[:, 4 + c2, :], mean_of[:, :], proj[:, 2 * c2:2 * c2 + 2, :],
                           start=True, stop=True).then_inc(gn_var, 1)
                    pe.wait_ge(sgu_out, CH // 2)
                    pe.wait_ge(gn_out, CH)
                for k in range(KD):
                    n = IN_TILES + k // 2
                    if k % 2 == 0:
                        pe.wait_ge(w_in_slot[n % WSLOTS], 16 * ((L * TILES + n) // WSLOTS + 1))
                    for b in range(BLOCKS):
                        for q in range(D // BANK):
                            last = mm(ps[:, 4 * b + q, :], yT[:, k, b * P:(b + 1) * P],
                                      oslot[n % WSLOTS][:, k % 2, q * BANK:(q + 1) * BANK],
                                      start=(k == 0), stop=(k == KD - 1))
                    if k % 2:
                        last.then_inc(w_free, 1)
                pe.wait_ge(w_free, WSLOTS + L * TILES + IN_TILES + OUT_TILES)

                transposes(2 * L + 1)
                project(L, IN_TILES + OUT_TILES, BANKS * L + IN_TILES)
                pe.wait_ge(tile_out, WSLOTS + BANKS * (L + 1))
                for b in range(BLOCKS):
                    for hd in range(HEADS):
                        o = ps[:, 4 * b + hd // 2, (hd % 2) * SEL:(hd % 2 + 1) * SEL]
                        last = mm(o, qT[:, hd, b * P:(b + 1) * P], subT[:, hd, :], start=True, stop=True)
                        if hd % 2:
                            last.then_inc(q_scored, 1)
                for b in range(BLOCKS):
                    pe.wait_ge(scores_out, (L + 1) * BLOCKS * HEADS // 2)
                    for q in range(D // BANK):
                        mm(ps[:, 4 * b + q, :], ident[:, :], h[:, b, q * BANK:(q + 1) * BANK],
                           start=True, stop=False)
                    rows = (L * BLOCKS + b) * HEADS * TOPK
                    with pe.Fori(0, HEADS) as i:
                        for j in range(TOPK):
                            pe.wait_ge(diag_done, i * TOPK + (rows + j + 1))
                            per = TOPK // VSLOTS
                            pe.wait_ge(v_in[j % VSLOTS],
                                       i * (16 * per) + 16 * (rows // VSLOTS + j // VSLOTS + 1))
                            for q in range(D // BANK):
                                last = mm(ps[:, 4 * b + q, :], diag[:, j, :],
                                          vslot[j % VSLOTS][:, q * BANK:(q + 1) * BANK], start=False, stop=False)
                            last.then_inc(v_free, 1)
                    for q in range(D // BANK):
                        last = mm(ps[:, 4 * b + q, :], zeros[:, :],
                                  zeros[:, 0:1].to_broadcast([P, BANK]), start=False, stop=True)
                    last.then_inc(block_done, 1)

        @block.scalar
        def _(act):
            a = nc.scalar.activation

            def norm_start(m):
                for b in range(BLOCKS):
                    a(zn[:, b, :], h[:, b, :], ACT.Square, accum_out=square_sum[:, b:b + 1]).then_inc(squared, 1)
                act.wait_ge(squared, BLOCKS * (m + 1))
                a(root[:, :], square_sum[:, :], ACT.Sqrt, scale=1.0 / D, bias=eps_col[:, :]).then_inc(rooted, 1)

            def norm_rows(m, gain_at):
                act.wait_ge(rstd_ready, m + 1)
                a(zn[:, 1, :], h[:, 1, :], ACT.Copy, scale=rstd[:, 1:2]).then_inc(zn_ready, 1)
                for kk in range(0, KD // 2, 2):
                    act.wait_ge(turned, (KD // 2) * m + kk + 1)
                    if kk == 0:
                        act.wait_ge(cols_ready, 3)
                    for k in (2 * kk, 2 * kk + 1):
                        a(zT[:, k, :], ps[:, kk % 4, (k % 2) * SEQ:(k % 2 + 1) * SEQ], ACT.Copy,
                          scale=colA[:, gain_at + k:gain_at + k + 1]).then_inc(zT_even, 1)

            act.wait_ge(made, CONSTANTS)
            act.wait_ge(params_turned, 1)
            a(colA[:, :], ps[:, 6, 0:ROWS_A], ACT.Copy).then_inc(cols_ready, 1)
            for s in range(2):
                a(convT[:, s * ROWS_B:(s + 1) * ROWS_B], ps[:, 6, (s + 1) * P:(s + 1) * P + ROWS_B], ACT.Copy)\
                    .then_inc(cols_ready, 1)
            act.wait_ge(x_in, 16 * BLOCKS)
            for L in range(LAYERS):
                norm_start(2 * L)
                norm_rows(2 * L, ROWS_MIX + KD * L)
                act.wait_ge(keys_turned, L + 1)
                for p2 in range(2):
                    rows = slice(64 * p2, 64 * p2 + 64)
                    a(subT[rows, :, p2 * NKEYS:(p2 + 1) * NKEYS],
                      ps[rows, 4:6, :].rearrange("p a (h n) -> p (a h) n", n=NKEYS), ACT.Copy).then_inc(keys_ready, 1)
                TD = WSLOTS + TILES * L
                if L == 0:
                    with act.Fori(0, 4) as i:
                        for t in range(WSLOTS):
                            wait_unfused(act, (w_free, i * WSLOTS + (WSLOTS + t + 1)))
                            a(proj[:, bass.ds(i * CH + 2 * t, 2), :],
                              ps[:, t, :].rearrange("p (c t) -> p c t", c=2), ACT.Copy).then_inc(tile_out, 1)
                    for gr in range(len(WINDOWS)):
                        act.wait_ge(pool_mixed, gr + 1)
                        for dd in range(2):
                            c = 2 * gr + dd
                            a(yT[:, c, :], ps[:, 4 + gr, dd * SEQ:(dd + 1) * SEQ], ACT.Copy,
                              scale=colA[:, ROWS_SCALE + c:ROWS_SCALE + c + 1]).then_inc(pool_out, 1)
                else:
                    act.wait_ge(sgu_turned, 1)
                    for s in range(2):
                        a(wmT[:, 4 * s:4 * s + 4, :], ps[:, 6 + s, :].rearrange("p (h t) -> p h t", h=4), ACT.Copy)\
                            .then_inc(sgu_copied, 1)
                    for i, func in enumerate((ACT.Copy, ACT.Sigmoid)):
                        for t in range(WSLOTS):
                            act.wait_ge(w_free, TD + i * WSLOTS + t + 1)
                            a(proj[:, i * CH + 2 * t:i * CH + 2 * t + 2, :],
                              ps[:, t, :].rearrange("p (c t) -> p c t", c=2), func).then_inc(tile_out, 1)
                    for t in range(WSLOTS):
                        act.wait_ge(w_free, TD + 2 * WSLOTS + t + 1)
                        for b in range(BLOCKS):
                            last = a(vt[:, b, t * WCOLS:(t + 1) * WCOLS], ps[:, t, b * WCOLS:(b + 1) * WCOLS],
                                     ACT.Gelu, accum_out=vsum[:, b, t:t + 1])
                        last.then_inc(tile_out, 1)
                    for t in range(WSLOTS):
                        act.wait_ge(w_free, TD + 3 * WSLOTS + t + 1)
                        a(proj[:, 2 * CH + 2 * t:2 * CH + 2 * t + 2, :],
                          ps[:, t, :].rearrange("p (c t) -> p c t", c=2), ACT.Gelu).then_inc(tile_out, 1)
                    act.wait_ge(v_centred, BLOCKS)
                    for b in range(BLOCKS):
                        a(padded[:, 4 * b:4 * b + 4, 0:SEQ], vt[:, b, :].rearrange("p (c t) -> p c t", c=4), ACT.Square,
                          accum_out=vstat[:, 1, b:b + 1]).then_inc(v_squared, 1)
                    act.wait_ge(v_squared, BLOCKS)
                    a(vstat[:, 2, :], vstat[:, 1, :], ACT.Sqrt, scale=1.0 / SECTION, bias=eps_col[:, :])\
                        .then_inc(v_root, 1)
                    for c2 in range(CH // 2):
                        act.wait_ge(gn_centred, c2 + 1)
                        a(proj[:, 2 * c2:2 * c2 + 2, :], proj[:, CH + 2 * c2:CH + 2 * c2 + 2, :], ACT.Square)\
                            .then_inc(gn_squared, 1)
                    for c2 in range(CH // 2):
                        act.wait_ge(gn_var, c2 + 1)
                        a(proj[:, 2 * c2:2 * c2 + 2, :], ps[:, 4 + c2, :].rearrange("p (c t) -> p c t", c=2),
                          ACT.Sqrt, bias=eps_col[:, :]).then_inc(gn_root, 1)
                    for c in range(CH):
                        act.wait_ge(gn_scaled, c // 2 + 1)
                        a(yT[:, CH + c, :], proj[:, CH + c, :], ACT.Silu,
                          scale=colA[:, ROWS_GNG + c:ROWS_GNG + c + 1],
                          bias=colA[:, ROWS_GNB + c:ROWS_GNB + c + 1]).then_inc(gn_out, 1)

                act.wait_ge(h_mixed, 8 * (L + 1))
                norm_start(2 * L + 1)
                norm_rows(2 * L + 1, ROWS_FFN + KD * L)
                for t in range(WSLOTS):
                    act.wait_ge(w_free, TD + IN_TILES + OUT_TILES + t + 1)
                    a(proj[:, 2 * t:2 * t + 2, :], ps[:, t, :].rearrange("p (c t) -> p c t", c=2), ACT.Copy)\
                        .then_inc(tile_out, 1)
                for b in range(BLOCKS):
                    for s in range(HEADS // 2):
                        act.wait_ge(q_scored, (L * BLOCKS + b) * HEADS // 2 + s + 1)
                        a(scores[:, b, 2 * s:2 * s + 2, :], ps[:, 4 * b + s, :].rearrange("p (h n) -> p h n", h=2),
                          ACT.Copy).then_inc(scores_out, 1)
                act.wait_ge(scores_out, (L + 1) * BLOCKS * HEADS // 2)
                for b in range(BLOCKS):
                    heads = (L * BLOCKS + b) * HEADS
                    with act.Fori(0, HEADS) as i:
                        wait_unfused(act, (experts_v, i + heads))
                        a(sc[:, :, :], scores[:, b, bass.ds(i, 1), :].rearrange("p a (x n) -> p (a x) n", x=2),
                          ACT.Copy).then_inc(head_in, 1)
                        act.wait_ge(under_max, i + (heads + 1))
                        a(expo[:, :], below[:, :], ACT.Exp, accum_out=denom[:, 0:1]).then_inc(exp_done, 1)
                        act.wait_ge(u_free, i * TOPK + (L * SLOTS_FREED_U + USLOTS + (b * HEADS + 1) * TOPK))
                        a(gelu[:, :], dots[:, :], ACT.Gelu).then_inc(gelu_done, 1)
                        act.wait_ge(weights_done, i + (heads + 1))
                        act.wait_ge(v_free, i * TOPK + (L * SLOTS_FREED_V + VSLOTS + b * HEADS * TOPK))
                        for j in range(TOPK):
                            a(diag[:, j, :], ident[:, :], ACT.Copy, scale=weight[:, j:j + 1]).then_inc(diag_done, 1)
                for b in range(BLOCKS):
                    act.wait_ge(block_done, L * BLOCKS + b + 1)
                    a(h[:, b, :], ps[:, 4 * b:4 * b + 4, :].rearrange("p a n -> p (a n)"), ACT.Copy)\
                        .then_inc(h_expert, 1)
                act.wait_ge(h_expert, BLOCKS * (L + 1))
            norm_start(2 * LAYERS)

        @block.vector
        def _(dve):
            v = nc.vector
            steps = [0]

            def step(ins):
                steps[0] += 1
                ins.then_inc(dve_step, 1)
                dve.wait_ge(dve_step, steps[0])

            def norm_scale(m):
                dve.wait_ge(rooted, m + 1)
                v.reciprocal(rstd[:, :], root[:, :]).then_inc(rstd_ready, 1)
                dve.wait_ge(rstd_ready, m + 1)

            def norm_rows(m, gain_at):
                norm_scale(m)
                v.tensor_scalar(zn[:, 0, :], h[:, 0, :], rstd[:, 0:1], None, ALU.mult).then_inc(zn_ready, 1)
                if m == 0:
                    dve.wait_ge(cols_ready, 3)
                for kk in range(1, KD // 2, 2):
                    dve.wait_ge(turned, (KD // 2) * m + kk + 1)
                    for k in (2 * kk, 2 * kk + 1):
                        v.tensor_scalar(zT[:, k, :], ps[:, kk % 4, (k % 2) * SEQ:(k % 2 + 1) * SEQ],
                                        colA[:, gain_at + k:gain_at + k + 1], None, ALU.mult).then_inc(zT_odd, 1)

            v.memset(token[:, 0:1], 0.0).then_inc(w_free, WSLOTS)
            v.memset(token[:, 1:2], 0.0).then_inc(tile_out, WSLOTS)
            dve.wait_ge(made, CONSTANTS)

            for L in range(LAYERS):
                norm_rows(2 * L, ROWS_MIX + KD * L)
                if L == 0:
                    step(v.memset(padpool[:, :, :, 0:WINDOWS[-1]], 0.0))
                    for gr, window in enumerate(WINDOWS):
                        step(v.tensor_scalar(inv_count[:, :], position[:, :], float(window), None, ALU.min))
                        step(v.reciprocal(inv_count[:, :], inv_count[:, :]))
                        dve.wait_ge(tile_out, WSLOTS + gr + 1)
                        own = proj[:, 2 * gr:2 * gr + 2, :]
                        W0 = WINDOWS[-1]
                        step(v.tensor_copy(padpool[:, 0, :, W0:], own))
                        lag, at = 1, 0
                        while lag < window:
                            step(v.tensor_tensor(padpool[:, 1 - at, :, W0:], padpool[:, at, :, W0:],
                                                 padpool[:, at, :, W0 - lag:W0 - lag + SEQ], ALU.add))
                            lag, at = 2 * lag, 1 - at
                        step(v.tensor_tensor(padpool[:, at, :, W0:], padpool[:, at, :, W0:],
                                             inv_count[:, None, :].to_broadcast([P, 2, SEQ]), ALU.mult))
                        v.tensor_tensor(own, padpool[:, at, :, W0:], own, ALU.subtract).then_inc(pooled, 1)
                    dve.wait_ge(pooled, len(WINDOWS))
                    edge = SHORT - 1
                    step(v.memset(padshort[:, :, 0:edge], 0.0))
                    for t in range(WSLOTS):
                        dve.wait_ge(tile_out, WSLOTS + 3 * WSLOTS + t + 1)
                        cs = slice(2 * t, 2 * t + 2)
                        step(v.tensor_tensor(padshort[:, cs, edge:], proj[:, 2 * CH + 2 * t:2 * CH + 2 * t + 2, :],
                                             proj[:, 3 * CH + 2 * t:3 * CH + 2 * t + 2, :], ALU.mult))
                        tap = lambda k, c: colA[:, ROWS_SHORT + k * CH + c:ROWS_SHORT + k * CH + c + 1]
                        acc = lambda c: proj[:, 2 * CH + c, :]
                        for c in (2 * t, 2 * t + 1):
                            step(v.tensor_scalar(acc(c), padshort[:, c, 0:SEQ], tap(0, c), None, ALU.mult))
                        for k in range(1, SHORT):
                            for c in (2 * t, 2 * t + 1):
                                step(v.scalar_tensor_tensor(acc(c), padshort[:, c, k:k + SEQ], tap(k, c), acc(c),
                                                            ALU.mult, ALU.add))
                        v.tensor_tensor(yT[:, CH + 2 * t:CH + 2 * t + 2, :], proj[:, CH + 2 * t:CH + 2 * t + 2, :],
                                        proj[:, 2 * CH + 2 * t:2 * CH + 2 * t + 2, :], ALU.mult).then_inc(conv_out, 2)
                else:
                    TB = WSLOTS + (IN_TILES + Q_TILES) * L
                    edge = TAPS - 1
                    step(v.memset(padded[:, :, 0:edge], 0.0))
                    for t in range(WSLOTS):
                        dve.wait_ge(tile_out, TB + WSLOTS + t + 1)
                        cs = slice(2 * t, 2 * t + 2)
                        step(v.tensor_tensor(padded[:, cs, edge:], proj[:, cs, :],
                                             proj[:, CH + 2 * t:CH + 2 * t + 2, :], ALU.mult))
                    for c in range(CH):
                        v.tensor_scalar(proj[:, c, :], padded[:, c, 0:SEQ], convT[:, c:c + 1],
                                        colA[:, ROWS_CONVB + c:ROWS_CONVB + c + 1], ALU.mult, ALU.add)\
                            .then_inc(conv_step, 1)
                    with dve.Fori(1, TAPS) as k:
                        for c in range(CH):
                            dve.wait_ge(conv_step, k * CH + (c + 1 - CH))
                            v.scalar_tensor_tensor(proj[:, c, :], padded[:, c, bass.ds(k, SEQ)],
                                                   convT[:, bass.ds(k * CH + c, 1)], proj[:, c, :],
                                                   ALU.mult, ALU.add).then_inc(conv_step, 1)
                    dve.wait_ge(tile_out, TB + 3 * WSLOTS)
                    dve.wait_ge(shared_in, 48)
                    step(v.tensor_reduce(vstat[:, 0, :], vsum[:, :, :], AX.X, ALU.add))
                    step(v.tensor_scalar(vstat[:, 0, :], vstat[:, 0, :], 1.0 / SECTION, None, ALU.mult))
                    for b in range(BLOCKS):
                        v.tensor_scalar(vt[:, b, :], vt[:, b, :], vstat[:, 0, b:b + 1], None, ALU.subtract)\
                            .then_inc(v_centred, 1)
                    dve.wait_ge(v_root, 1)
                    step(v.reciprocal(vstat[:, 3, :], vstat[:, 2, :]))
                    for b in range(BLOCKS):
                        step(v.scalar_tensor_tensor(vt[:, b, :], vt[:, b, :], vstat[:, 3, b:b + 1], vgb[:, 0, :],
                                                    ALU.mult, ALU.mult))
                        v.tensor_tensor(vt[:, b, :], vt[:, b, :], vgb[:, 1, :], ALU.add).then_inc(v_ready, 1)
                    for c2 in range(CH // 2):
                        cs = slice(2 * c2, 2 * c2 + 2)
                        dve.wait_ge(gn_mean, c2 + 1)
                        v.tensor_tensor(proj[:, CH + 2 * c2:CH + 2 * c2 + 2, :], proj[:, cs, :],
                                        ps[:, 4 + c2, :].rearrange("p (c t) -> p c t", c=2), ALU.subtract)\
                            .then_inc(gn_centred, 1)
                    for c2 in range(CH // 2):
                        dve.wait_ge(gated, c2 + 1)
                        v.tensor_tensor(yT[:, 2 * c2:2 * c2 + 2, :], proj[:, 2 * CH + 2 * c2:2 * CH + 2 * c2 + 2, :],
                                        ps[:, c2, :].rearrange("p (c t) -> p c t", c=2), ALU.mult)\
                            .then_inc(sgu_out, 1)
                    for c2 in range(CH // 2):
                        cs = slice(2 * c2, 2 * c2 + 2)
                        zs = slice(CH + 2 * c2, CH + 2 * c2 + 2)
                        dve.wait_ge(gn_root, c2 + 1)
                        step(v.reciprocal(proj[:, cs, :], proj[:, cs, :]))
                        v.tensor_tensor(proj[:, zs, :], proj[:, zs, :], proj[:, cs, :], ALU.mult)\
                            .then_inc(gn_scaled, 1)

                dve.wait_ge(w_free, WSLOTS + L * TILES + IN_TILES + OUT_TILES)
                for b in range(BLOCKS):
                    for q in range(D // BANK):
                        s = slice(q * BANK, (q + 1) * BANK)
                        v.tensor_tensor(h[:, b, s], ps[:, 4 * b + q, :], h[:, b, s], ALU.add).then_inc(h_mixed, 1)
                norm_rows(2 * L + 1, ROWS_FFN + KD * L)
                dve.wait_ge(gain_in, 16 * (L + 1))
                for b in range(BLOCKS):
                    v.tensor_tensor(zn[:, b, :], zn[:, b, :], gB[:, :], ALU.mult).then_inc(xn_ready, 1)

                dve.wait_ge(xn_ready, BLOCKS * (L + 1))
                dve.wait_ge(q_scored, (L + 1) * BLOCKS * HEADS // 2)
                v.memset(token[:, 2 * L + 2:2 * L + 3], 0.0).then_inc(u_free, USLOTS)
                v.memset(token[:, 2 * L + 3:2 * L + 4], 0.0).then_inc(v_free, VSLOTS)
                for b in range(BLOCKS):
                    heads = (L * BLOCKS + b) * HEADS
                    with dve.Fori(0, HEADS) as i:
                        n = [0]

                        def routed(ins, unfused=False):
                            n[0] += 1
                            ins.then_inc(route_step, 1)
                            value = i * ROUTE_STEPS + (heads * ROUTE_STEPS + n[0])
                            if unfused:
                                wait_unfused(dve, (route_step, value))
                            else:
                                dve.wait_ge(route_step, value)

                        def top16(values, spare, best_, besti_):
                            routed(v.max(best_[0], values), True)
                            routed(v.max_index(besti_[0], best_[0], values), True)
                            routed(v.match_replace(spare, best_[0], values, LOWEST), True)
                            routed(v.max(best_[1], spare), True)
                            routed(v.max_index(besti_[1], best_[1], spare), True)

                        wait_unfused(dve, (head_in, i + (heads + 1)))
                        for p2 in range(2):
                            halves = [slice(0, 8), slice(8, 16)]
                            top16(sc[:, p2, :], sc2[:, p2, :], [top[:, p2, x] for x in halves],
                                  [topi[:, p2, x] for x in halves])
                        routed(v.tensor_scalar(topf[:, 0, :], topi[:, 0, :], float(NKEYS * L), None, ALU.add))
                        routed(v.tensor_copy(topf[:, 1, :], topi[:, 1, :]))
                        routed(v.tensor_tensor(cand[:, :, :], top[:, 0, :, None].to_broadcast([P, TOPK, TOPK]),
                                               top[:, 1, None, :].to_broadcast([P, TOPK, TOPK]), ALU.add), True)
                        flat = cand[:, :, :].rearrange("p a b -> p (a b)")
                        top16(flat, cand2[:, :], [best[:, x] for x in halves], [besti[:, x] for x in halves])
                        v.tensor_scalar(below[:, :], best[:, :], best[:, 0:1], None, ALU.subtract)\
                            .then_inc(under_max, 1)
                        routed(v.tensor_scalar(pos[:, 0, :], besti[:, :], 4, None, ALU.logical_shift_right))
                        routed(v.tensor_scalar(pos[:, 1, :], besti[:, :], TOPK - 1, None, ALU.bitwise_and))
                        for p2 in range(2):
                            o = onehot[:, p2, :, :]
                            routed(v.tensor_tensor(o, pos[:, p2, :, None].to_broadcast([P, TOPK, TOPK]),
                                                   iota16[:, None, :].to_broadcast([P, TOPK, TOPK]), ALU.is_equal))
                            routed(v.tensor_tensor(o, o, topf[:, p2, None, :].to_broadcast([P, TOPK, TOPK]),
                                                   ALU.mult))
                            routed(v.tensor_reduce(key[:, p2, :], o, AX.X, ALU.add))
                        v.scalar_tensor_tensor(expert_u[:, :], key[:, 0, :], float(NKEYS), key[:, 1, :],
                                               ALU.mult, ALU.add).then_inc(experts_u, 1)
                        dve.wait_ge(exp_done, i + (heads + 1))
                        routed(v.reciprocal(denom[:, 1:2], denom[:, 0:1]))
                        routed(v.tensor_scalar(gates[:, :], expo[:, :], denom[:, 1:2], None, ALU.mult))
                        for slot_in in v_in:
                            dve.wait_ge(slot_in, (i + heads) * (16 * TOPK // VSLOTS))
                        v.scalar_tensor_tensor(expert_v[:, :], key[:, 0, :], float(NKEYS), key[:, 1, :],
                                               ALU.mult, ALU.add).then_inc(experts_v, 1)
                        assert n[0] == ROUTE_STEPS, n
                        for j in range(TOPK):
                            slot = uslot[j % USLOTS]
                            per = TOPK // USLOTS
                            dve.wait_ge(u_in[j % USLOTS],
                                        i * (16 * per) + 16 * (heads * per + j // USLOTS + 1))
                            v.tensor_tensor_reduce(out=slot, in0=slot, in1=zn[:, b, :], scale=1.0, scalar=0.0,
                                                   op0=ALU.mult, op1=ALU.add,
                                                   accum_out=dots[:, j:j + 1]).then_inc(u_free, 1)
                        dve.wait_ge(gelu_done, i + (heads + 1))
                        dve.wait_ge(diag_done, (i + heads) * TOPK)
                        v.tensor_tensor(weight[:, :], gelu[:, :], gates[:, :], ALU.mult).then_inc(weights_done, 1)

            norm_scale(2 * LAYERS)
            dve.wait_ge(gain_in, 16 * (LAYERS + 1))
            for b in range(BLOCKS):
                v.scalar_tensor_tensor(zn[:, b, :], h[:, b, :], rstd[:, b:b + 1], gB[:, :],
                                       ALU.mult, ALU.mult).then_inc(result_ready, 1)


ROUTE_STEPS = 28

_INS = ['x', 'mix_norm_g', 'ffn_norm_g', 'ev_w_in', 'ev_pool_w', 'ev_pool_scale', 'ev_conv_w', 'ev_w_out',
        'od_w_in', 'od_v_norm_g', 'od_v_norm_b', 'od_sgu_w', 'od_sgu_b', 'od_conv_w', 'od_conv_b',
        'od_gn_g', 'od_gn_b', 'od_w_out', 'peer_w_q', 'peer_subkeys', 'peer_u', 'peer_v', 'final_norm_g']


def kernel(**inputs):
    import numpy as np
    import concourse.bacc as bacc
    from concourse import mybir as mb
    from concourse.bass_utils import run_bass_kernel_spmd as run

    nc = bacc.Bacc("TRN2", target_bir_lowering=False, num_devices=1)
    arrays, args = {}, []
    for name in _INS:
        a = np.ascontiguousarray(inputs[name])
        arrays[f"in_{name}"] = a
        args.append(nc.dram_tensor(f"in_{name}", a.shape, mb.dt.from_np(a.dtype), kind="ExternalInput").ap())
    args.append(nc.dram_tensor("out", (1, SEQ, D), mb.dt.float32, kind="ExternalOutput").ap())
    two_layers(nc, *args)
    return run(nc, [arrays], core_ids=[0]).results[0]["out"]
```

```python
from contextlib import ExitStack

import concourse.bass as bass
from concourse import mybir

F32 = mybir.dt.float32
F32R = mybir.dt.float32r
I32 = mybir.dt.int32
U32 = mybir.dt.uint32
ALU = mybir.AluOpType
ACT = mybir.ActivationFunctionType
AX = mybir.AxisListType

P = 128
D = 2048
SEQ = 256
BLOCKS = SEQ // P
KD = D // P
LAYERS = 2
BANK = 512
WCOLS = 256
SECTION = 4 * WCOLS
CH = SECTION // P
PART = 1024
QUARTERS = 4
RAW = 8
PAIRS = 4
IN_GROUPS, OUT_GROUPS, Q_GROUPS = 16, 8, 4
GROUPS = IN_GROUPS + OUT_GROUPS + Q_GROUPS
PARTS = GROUPS * QUARTERS
BANKS = IN_GROUPS + Q_GROUPS
WINDOWS = (2, 4, 8, 16)
SHORT = 3
TAPS = 31
HEADS = 8
TOPK = 16
NKEYS = 128
SEL = 2 * NKEYS
USLOTS, VSLOTS = 4, 8
EPS = 1e-6
LOWEST = -3.0e38

ROWS_MIX, ROWS_FFN, ROWS_SCALE, ROWS_SHORT = 0, 32, 64, 72
ROWS_CONVB, ROWS_GNG, ROWS_GNB, ROWS_A = 96, 104, 112, 120
ROWS_B = TAPS * CH // 2


def two_layers(nc, x, mix_norm_g, ffn_norm_g, ev_w_in, ev_pool_w, ev_pool_scale, ev_conv_w, ev_w_out,
               od_w_in, od_v_norm_g, od_v_norm_b, od_sgu_w, od_sgu_b, od_conv_w, od_conv_b,
               od_gn_g, od_gn_b, od_w_out, peer_w_q, peer_subkeys, peer_u, peer_v, final_norm_g, out):
    w_in = (ev_w_in[0], od_w_in[0])
    w_out = (ev_w_out[0], od_w_out[0])
    by_rows = lambda w: w.rearrange("(k p) c -> p k c", p=P)
    chunked = lambda v: v.rearrange("(r c) -> r c", c=P)

    with ExitStack() as ctx:
        sb = lambda name, shape, dt=F32: ctx.enter_context(nc.sbuf_tensor(name, shape, dt))
        sem = lambda name: ctx.enter_context(nc.semaphore(name))

        h = sb("h", [P, BLOCKS, D])
        zn = sb("zn", [P, BLOCKS, D])
        with ExitStack() as early:
            esb = lambda name, shape, dt=F32: early.enter_context(nc.sbuf_tensor(name, shape, dt))
            raw = esb("raw", [P, RAW, PART])
            w_high = esb("w_high", [P, PAIRS, PART], F32R)
            w_low = esb("w_low", [P, PAIRS, PART], F32R)
        vring = sb("vring", [P, VSLOTS, D])
        qT = sb("qT", [P, CH, SEQ])
        proj = sb("proj", [P, 4 * CH, SEQ])
        vt = proj[:, 3 * CH:4 * CH, :].rearrange("p k t -> p (k t)").rearrange("p (b c) -> p b c", b=BLOCKS)
        uring = proj[:, :, :].rearrange("p (s k) t -> p s (k t)", s=USLOTS)
        with ExitStack() as early:
            zT_high = early.enter_context(nc.sbuf_tensor("zT_high", [P, KD, SEQ], F32R))
        scores = sb("scores", [P, BLOCKS, HEADS, SEL])
        zT_low = sb("zT_low", [P, KD, SEQ], F32R)
        paramrow = proj[:, 0:2, :].rearrange("p k t -> p (k t)")[:, 0:3 * P].rearrange("p (a c) -> p a c", a=3)
        uslot = [uring[:, k, :] for k in range(USLOTS)]
        vslot = [vring[:, k, :] for k in range(VSLOTS)]
        gB = sb("gB", [P, D])
        sgub = gB[0:1, 0:HEADS * P]
        wmT = gB[:, HEADS * P:2 * HEADS * P].rearrange("p (h t) -> p h t", h=HEADS)
        inv_count, position = gB[:, 0:SEQ], gB[:, SEQ:2 * SEQ]
        shared = sb("shared", [P, 2 * SECTION])
        poolw = shared[:, :].rearrange("p (k d) -> p k d", d=WCOLS)
        vgb = shared[:, :].rearrange("p (a c) -> p a c", a=2)
        subT = sb("subT", [P, HEADS, SEL])
        scratch = sb("scratch", [P, CH * (SEQ + TAPS - 1)])
        subraw = scratch[:, 0:HEADS * P].rearrange("p (h k) -> p h k", h=HEADS)
        sguraw = scratch[:, HEADS * P:2 * HEADS * P].rearrange("p (h s) -> p h s", h=HEADS)
        padded = scratch[:, :].rearrange("p (c t) -> p c t", c=CH)
        SP_ = SEQ + SHORT - 1
        padshort = scratch[:, 0:CH * SP_].rearrange("p (c t) -> p c t", c=CH)
        WP = SEQ + WINDOWS[-1]
        padpool = scratch[:, 0:4 * WP].rearrange("p (a c t) -> p a c t", a=2, c=2)
        diag = scratch[:, 0:TOPK * P].rearrange("p (j c) -> p j c", c=P)
        ident = sb("ident", [P, P])
        mean_of = sb("mean_of", [P, P])
        ones_row = sb("ones_row", [1, P])
        zeros = sb("zeros", [P, P], mybir.dt.bfloat16)
        eps_col = sb("eps_col", [P, 1])
        colA = sb("colA", [P, ROWS_A])
        convT = sb("convT", [P, TAPS * CH])
        iota16 = sb("iota16", [P, TOPK])
        square_sum = sb("square_sum", [P, BLOCKS])
        root = sb("root", [P, BLOCKS])
        rstd = sb("rstd", [P, BLOCKS])
        vsum = sb("vsum", [P, BLOCKS, 4])
        vstat = sb("vstat", [P, 4, BLOCKS])
        grid = lambda at, a: shared[:, at:at + a * SEL]
        sc = grid(0, 1).rearrange("p (x n) -> p x n", x=2)
        sc2 = grid(SEL, 1).rearrange("p (x n) -> p x n", x=2)
        cand = grid(2 * SEL, 1).rearrange("p (a b) -> p a b", a=TOPK)
        cand2 = grid(3 * SEL, 1)
        onehot = grid(4 * SEL, 2).rearrange("p (x a b) -> p x a b", x=2, a=TOPK)
        top = sb("top", [P, 2, TOPK])
        topi = sb("topi", [P, 2, TOPK], U32)
        topf = sb("topf", [P, 2, TOPK])
        best = sb("best", [P, TOPK])
        besti = sb("besti", [P, TOPK], U32)
        pos = sb("pos", [P, 2, TOPK], U32)
        key = sb("key", [P, 2, TOPK])
        below = sb("below", [P, TOPK])
        expo = sb("expo", [P, TOPK])
        denom = sb("denom", [P, 2])
        gates = sb("gates", [P, TOPK])
        expert_u = sb("expert_u", [P, TOPK], I32)
        expert_v = sb("expert_v", [P, TOPK], I32)
        dots = sb("dots", [P, TOPK])
        gelu = sb("gelu", [P, TOPK])
        weight = sb("weight", [P, TOPK])
        token = sb("token", [P, 4 + LAYERS])
        freed = sb("freed", [P, LAYERS])
        ps = ctx.enter_context(nc.psum_tensor("ps", [P, 8, BANK], F32))

        made = sem("made")
        x_in = sem("x_in")
        rows_in = sem("rows_in")
        gain_in = sem("gain_in")
        shared_in = sem("shared_in")
        keys_in = sem("keys_in")
        sgu_in = sem("sgu_in")
        raw_in = [sem(f"raw_in{s}") for s in range(RAW)]
        high_done = sem("high_done")
        low_done = sem("low_done")
        pair_free = sem("pair_free")
        squared = sem("squared")
        rooted = sem("rooted")
        rstd_ready = sem("rstd_ready")
        zn_ready = sem("zn_ready")
        turned = sem("turned")
        zT_rounded = sem("zT_rounded")
        zT_split = sem("zT_split")
        xn_ready = sem("xn_ready")
        params_turned = sem("params_turned")
        cols_ready = sem("cols_ready")
        keys_turned = sem("keys_turned")
        keys_ready = sem("keys_ready")
        sgu_turned = sem("sgu_turned")
        sgu_copied = sem("sgu_copied")
        sgu_masked = sem("sgu_masked")
        tile_out = sem("tile_out")
        pooled = sem("pooled")
        pool_mixed = sem("pool_mixed")
        conv_out = sem("conv_out")
        y_rounded = sem("y_rounded")
        y_split = sem("y_split")
        conv_step = sem("conv_step")
        v_squared = sem("v_squared")
        v_centred = sem("v_centred")
        v_root = sem("v_root")
        v_ready = sem("v_ready")
        gn_mean = sem("gn_mean")
        gn_centred = sem("gn_centred")
        gn_squared = sem("gn_squared")
        gn_var = sem("gn_var")
        gn_root = sem("gn_root")
        gn_scaled = sem("gn_scaled")
        gn_out = sem("gn_out")
        gated = sem("gated")
        sgu_out = sem("sgu_out")
        h_mixed = sem("h_mixed")
        q_scored = sem("q_scored")
        scores_out = sem("scores_out")
        head_in = sem("head_in")
        under_max = sem("under_max")
        exp_done = sem("exp_done")
        experts_u = sem("experts_u")
        experts_v = sem("experts_v")
        u_in = [sem(f"u_in{s}") for s in range(USLOTS)]
        v_in = [sem(f"v_in{s}") for s in range(VSLOTS)]
        u_free = sem("u_free")
        v_free = sem("v_free")
        gelu_done = sem("gelu_done")
        weights_done = sem("weights_done")
        diag_done = sem("diag_done")
        block_done = sem("block_done")
        h_expert = sem("h_expert")
        result_ready = sem("result_ready")
        stored = sem("stored")
        dve_step = sem("dve_step")
        route_step = sem("route_step")

        SLOTS_FREED_U = USLOTS + BLOCKS * HEADS * TOPK
        SLOTS_FREED_V = VSLOTS + BLOCKS * HEADS * TOPK
        CONSTANTS = 9
        Q_AT = PARTS - Q_GROUPS * QUARTERS

        ROW_ORDER = (((0, 0), (CH, CH)), ((CH, 0), (0, CH)))

        block = ctx.enter_context(nc.Block())

        def wait_unfused(eng, *waits):
            if all(isinstance(value, int) for _, value in waits):
                for s, value in waits:
                    eng.wait_ge(s, value)
                return
            for _, value in waits:
                eng.to_reg(value)
            eng.wait_ge(made, CONSTANTS)
            for s, value in waits:
                eng.wait_ge(s, value)

        @block.sync
        def _(sp):
            for b in range(BLOCKS):
                sp.dma_start(h[:, b, :], x[0, b * P:(b + 1) * P, :]).then_inc(x_in, 16)
            rows = paramrow
            sp.dma_start(rows[ROWS_MIX:ROWS_MIX + 32, 0, :],
                         mix_norm_g.rearrange("l (k c) -> (l k) c", c=P)).then_inc(rows_in, 16)
            sp.dma_start(rows[ROWS_FFN:ROWS_FFN + 32, 0, :],
                         ffn_norm_g.rearrange("l (k c) -> (l k) c", c=P)).then_inc(rows_in, 16)
            sp.dma_start(rows[ROWS_SCALE:ROWS_SCALE + CH, 0, :], chunked(ev_pool_scale[0])).then_inc(rows_in, 16)
            sp.dma_start(rows[ROWS_SHORT:ROWS_SHORT + SHORT * CH, 0, :],
                         ev_conv_w[0].rearrange("k (r c) -> (k r) c", c=P)).then_inc(rows_in, 16)
            sp.dma_start(rows[ROWS_CONVB:ROWS_CONVB + CH, 0, :], chunked(od_conv_b[0])).then_inc(rows_in, 16)
            sp.dma_start(rows[ROWS_GNG:ROWS_GNG + CH, 0, :], chunked(od_gn_g[0])).then_inc(rows_in, 16)
            sp.dma_start(rows[ROWS_GNB:ROWS_GNB + CH, 0, :], chunked(od_gn_b[0])).then_inc(rows_in, 16)
            taps = od_conv_w[0].rearrange("k (r c) -> (k r) c", c=P)
            sp.dma_start(rows[0:ROWS_B, 1, :], taps[0:ROWS_B, :]).then_inc(rows_in, 16)
            sp.dma_start(rows[0:ROWS_B, 2, :], taps[ROWS_B:2 * ROWS_B, :]).then_inc(rows_in, 16)

            def load_part(slot, n, src):
                sp.wait_ge(low_done, n + 1)
                sp.dma_start(raw[:, slot, :].rearrange("p (k c) -> p k c", c=src.shape[-1]), src)\
                  .then_inc(raw_in[slot], 16)

            for L in range(LAYERS):
                win, wout, wq = by_rows(w_in[L]), by_rows(w_out[L]), by_rows(peer_w_q[L])
                if L:
                    sp.wait_ge(h_expert, BLOCKS * L)
                sp.dma_start(subraw.rearrange("n h (p k) -> n h p k", p=2),
                             peer_subkeys[L].rearrange("h p n k -> n h p k")).then_inc(keys_in, 16)
                if L == 0:
                    sp.dma_start(poolw, ev_pool_w[0].rearrange("g (k p) d -> p (g k) d", p=P))\
                      .then_inc(shared_in, 16)
                else:
                    sp.dma_start(sguraw, od_sgu_w[0].rearrange("h t s -> t h s")).then_inc(sgu_in, 16)
                    sp.dma_start(sgub, od_sgu_b[0:1].rearrange("o h t -> o (h t)")).then_inc(sgu_in, 16)
                    sp.dma_start(vgb[:, 0, :], od_v_norm_g[0:1, :].to_broadcast([P, SECTION]))\
                      .then_inc(shared_in, 16)
                    sp.dma_start(vgb[:, 1, :], od_v_norm_b[0:1, :].to_broadcast([P, SECTION]))\
                      .then_inc(shared_in, 16)
                GQ = 4 * QUARTERS
                if L == 0:
                    with sp.Fori(0, 4) as i:
                        for m in range(GQ):
                            t, q = divmod(m, QUARTERS)
                            load_part(m % RAW, i * GQ + m,
                                      win[:, 4 * q:4 * q + 4, bass.ds(i * SECTION + t * WCOLS, WCOLS)])
                else:
                    order = [(2 + t % 2, t // 2) for t in range(8)] + [(1, t) for t in range(4)] + [(0, t) for t in range(4)]
                    for m in range(IN_GROUPS * QUARTERS):
                        group, q = divmod(m, QUARTERS)
                        part, t = order[group]
                        at = part * SECTION + t * WCOLS
                        load_part(m % RAW, L * PARTS + m, win[:, 4 * q:4 * q + 4, at:at + WCOLS])
                for first, n in ROW_ORDER[L]:
                    with sp.Fori(0, CH // (RAW // 2)) as i:
                        for m in range(RAW):
                            load_part(m, i * RAW + (L * PARTS + IN_GROUPS * QUARTERS + 2 * n + m),
                                      wout[:, bass.ds(i * (RAW // 2) + (first + m // 2), 1),
                                           (m % 2) * PART:(m % 2 + 1) * PART])
                for m in range(Q_GROUPS * QUARTERS):
                    t, q = divmod(m, QUARTERS)
                    load_part(m % RAW, L * PARTS + Q_AT + m, wq[:, 4 * q:4 * q + 4, t * WCOLS:(t + 1) * WCOLS])
                if L:
                    sp.wait_ge(sgu_out, CH // 2)
                else:
                    sp.wait_ge(pooled, len(WINDOWS))
                sp.dma_start(gB[:, :], ffn_norm_g[L:L + 1, :].to_broadcast([P, D])).then_inc(gain_in, 16)
            sp.wait_ge(xn_ready, BLOCKS * LAYERS)
            sp.dma_start(gB[:, :], final_norm_g.rearrange("(a c) -> a c", a=1).to_broadcast([P, D]))\
              .then_inc(gain_in, 16)
            for b in range(BLOCKS):
                sp.wait_ge(result_ready, b + 1)
                sp.dma_start(out[0, b * P:(b + 1) * P, :], zn[:, b, :]).then_inc(stored, 16)
            sp.wait_ge(stored, 16 * BLOCKS)

        @block.gpsimd
        def _(pool):
            g = nc.gpsimd
            g.memset(ident[:, :], 0.0).then_inc(made, 1)
            g.memset(mean_of[:, :], 1.0 / P).then_inc(made, 1)
            g.memset(ones_row[:, :], 1.0).then_inc(made, 1)
            g.memset(zeros[:, :], 0.0).then_inc(made, 1)
            g.memset(eps_col[:, :], EPS).then_inc(made, 1)
            g.memset(subT[:, :, :], 0.0).then_inc(made, 1)
            g.iota(position[:, :], pattern=[[1, SEQ]], base=1, channel_multiplier=0,
                   allow_small_or_imprecise_dtypes=True).then_inc(made, 1)
            g.iota(iota16[:, :], pattern=[[1, TOPK]], base=0, channel_multiplier=0,
                   allow_small_or_imprecise_dtypes=True).then_inc(made, 1)
            pool.wait_ge(made, 1)
            g.affine_select(out=ident[:, :], in_=ident[:, :], compare_op=ALU.not_equal, fill=1.0, base=0,
                            pattern=[[-1, P]], channel_multiplier=1).then_inc(made, 1)

            def low_half(m, n):
                pool.wait_ge(high_done, n + 1)
                g.tensor_tensor(w_low[:, m % PAIRS, :], raw[:, m, :], w_high[:, m % PAIRS, :].bitcast(F32),
                                ALU.subtract).then_inc(low_done, 1)

            def low_halves(L):
                with pool.Fori(0, PARTS // RAW - 1) as i:
                    for m in range(RAW):
                        low_half(m, i * RAW + (L * PARTS + m))
                for m in range(RAW - QUARTERS):
                    low_half(m, (L + 1) * PARTS - RAW + m)

            def gather_u(L, b, i, j):
                listed = [(experts_u, i + ((L * BLOCKS + b) * HEADS + 2))] if j == 0 else []
                freed = L * SLOTS_FREED_U + b * HEADS * TOPK
                wait_unfused(pool, *listed, (u_free, i * TOPK + (freed + j + 1)))
                g.indirect_dma_start(
                    out=uslot[j % USLOTS], out_offset=None, in_=peer_u.rearrange("l e d -> (l e) d"),
                    in_offset=bass.IndirectOffsetOnAxis(ap=expert_u[:, j:j + 1], axis=0),
                ).then_inc(u_in[j % USLOTS], 16)

            def gather_v(L, b, i, j):
                listed = [(experts_v, i + ((L * BLOCKS + b) * HEADS + 1))] if j == 0 else []
                freed = L * SLOTS_FREED_V + b * HEADS * TOPK
                wait_unfused(pool, *listed, (v_free, i * TOPK + (freed + j + 1)))
                g.indirect_dma_start(
                    out=vslot[j % VSLOTS], out_offset=None, in_=peer_v.rearrange("l e d -> (l e) d"),
                    in_offset=bass.IndirectOffsetOnAxis(ap=expert_v[:, j:j + 1], axis=0),
                ).then_inc(v_in[j % VSLOTS], 16)

            def experts(L):
                for j in range(TOPK):
                    gather_u(L, 0, 0, j)
                    if j < QUARTERS:
                        low_half(RAW - QUARTERS + j, (L + 1) * PARTS - QUARTERS + j)
                for j in range(TOPK):
                    gather_v(L, 0, 0, j)
                for b in range(BLOCKS):
                    with pool.Fori(1 - b, HEADS) as i:
                        for j in range(TOPK):
                            gather_u(L, b, i, j)
                        for j in range(TOPK):
                            gather_v(L, b, i, j)

            low_halves(0)
            experts(0)
            pool.wait_ge(sgu_in, 32)
            g.affine_select(out=sguraw, in_=sguraw, compare_op=ALU.is_ge, fill=0.0, base=0,
                            pattern=[[0, HEADS], [-1, P]], channel_multiplier=1).then_inc(sgu_masked, 1)
            low_halves(1)
            experts(1)

        @block.tensor
        def _(pe):
            mm = nc.tensor.matmul

            def transposes(m):
                pe.wait_ge(zn_ready, BLOCKS * (m + 1))
                for kk in range(KD // 2):
                    if kk >= 4:
                        pe.wait_ge(zT_split, (KD // 2) * m + kk - 4 + 1)
                    for k in (2 * kk, 2 * kk + 1):
                        for b in range(BLOCKS):
                            at = (k % 2) * SEQ + b * P
                            last = nc.tensor.transpose(ps[:, kk % 4, at:at + P], zn[:, b, k * P:(k + 1) * P],
                                                       ident[:, :])
                    last.then_inc(turned, 1)
                pe.wait_ge(zT_split, (KD // 2) * (m + 1))

            def three_passes(o, left, right, start, stop):
                mm(o, left[0], right[0], start=start, stop=False)
                mm(o, left[0], right[1], start=False, stop=False)
                return mm(o, left[1], right[0], start=False, stop=stop)

            def channel_bank(t, parts_before, i=0):
                for q in range(QUARTERS):
                    high, low = (w[:, q, :].rearrange("p (k c) -> p k c", c=WCOLS) for w in (w_high, w_low))
                    pe.wait_ge(low_done, i + (parts_before + q + 1))
                    for c in range(WCOLS // P):
                        cs = slice(c * P, (c + 1) * P)
                        for k in range(4):
                            kz = 4 * q + k
                            last = three_passes(ps[:, t, c * SEQ:(c + 1) * SEQ],
                                                (high[:, k, cs], low[:, k, cs]),
                                                (zT_high[:, kz, :], zT_low[:, kz, :]),
                                                start=(q == 0 and c == 0 and k == 0),
                                                stop=(q == QUARTERS - 1 and c == 1 and k == 3))
                    last.then_inc(pair_free, 1)

            def project(L, group, banks, sections=1):
                parts = RAW + L * PARTS + group * QUARTERS
                if sections == 1:
                    for t in range(4):
                        pe.wait_ge(tile_out, banks + t + 1)
                        channel_bank(t, parts + t * QUARTERS)
                else:
                    with pe.Fori(0, sections) as i:
                        for t in range(4):
                            pe.wait_ge(tile_out, i * 4 + (banks + t + 1))
                            channel_bank(t, parts + t * QUARTERS, i * 4 * QUARTERS)

            pe.wait_ge(made, CONSTANTS)
            pe.wait_ge(rows_in, 16 * 9)
            nc.tensor.transpose(ps[:, 6, 0:ROWS_A], paramrow[0:ROWS_A, 0, :], ident[0:ROWS_A, 0:ROWS_A])
            for a in range(2):
                last = nc.tensor.transpose(ps[:, 6, (a + 1) * P:(a + 1) * P + ROWS_B], paramrow[0:ROWS_B, a + 1, :],
                                           ident[0:ROWS_B, 0:ROWS_B])
            last.then_inc(params_turned, 1)

            for L in range(LAYERS):
                transposes(2 * L)
                pe.wait_ge(keys_in, 16 * (L + 1))
                for hd in range(HEADS):
                    last = nc.tensor.transpose(ps[:, 4 + hd // 4, (hd % 4) * P:(hd % 4 + 1) * P], subraw[:, hd, :],
                                               ident[:, :])
                last.then_inc(keys_turned, 1)
                if L == 0:
                    project(L, 0, 0, 4)
                    pe.wait_ge(shared_in, 16)
                    pe.wait_ge(keys_ready, 2)
                    for gr in range(len(WINDOWS)):
                        pe.wait_ge(pooled, gr + 1)
                        for dd in range(2):
                            for kc in range(2):
                                last = mm(ps[:, 4 + gr, dd * SEQ:(dd + 1) * SEQ],
                                          poolw[:, 2 * gr + kc, dd * P:(dd + 1) * P], proj[:, 2 * gr + kc, :],
                                          start=(kc == 0), stop=(kc == 1))
                        last.then_inc(pool_mixed, 1)
                else:
                    pe.wait_ge(sgu_masked, 1)
                    for hd in range(HEADS):
                        last = nc.tensor.transpose(ps[:, 6 + hd // 4, (hd % 4) * P:(hd % 4 + 1) * P],
                                                   sguraw[:, hd, :], ident[:, :])
                    last.then_inc(sgu_turned, 1)
                    bank0 = BANKS * L
                    project(L, 0, bank0, 2)
                    for t in range(4):
                        pe.wait_ge(tile_out, bank0 + 8 + t + 1)
                        for q in range(QUARTERS):
                            high, low = (w[:, q, :].rearrange("p (k c) -> p k c", c=WCOLS) for w in (w_high, w_low))
                            pe.wait_ge(low_done, RAW + L * PARTS + (8 + t) * QUARTERS + q + 1)
                            for b in range(BLOCKS):
                                for k in range(4):
                                    kz = 4 * q + k
                                    last = three_passes(ps[:, t, b * WCOLS:(b + 1) * WCOLS],
                                                        (zT_high[:, kz, b * P:(b + 1) * P],
                                                         zT_low[:, kz, b * P:(b + 1) * P]),
                                                        (high[:, k, :], low[:, k, :]),
                                                        start=(q == 0 and b == 0 and k == 0),
                                                        stop=(q == QUARTERS - 1 and b == 1 and k == 3))
                            last.then_inc(pair_free, 1)
                    pe.wait_ge(conv_step, TAPS * CH)
                    pe.wait_ge(keys_ready, 4)
                    pe.wait_ge(sgu_copied, 2)
                    for c2 in range(CH // 2):
                        mm(ps[:, 4 + c2, :], mean_of[:, :], proj[:, 2 * c2:2 * c2 + 2, :],
                           start=True, stop=True).then_inc(gn_mean, 1)
                    for t in range(4):
                        pe.wait_ge(tile_out, bank0 + 12 + t + 1)
                        channel_bank(t, RAW + L * PARTS + (12 + t) * QUARTERS)
                        if t == 1:
                            for c2 in range(CH // 2):
                                pe.wait_ge(gn_squared, c2 + 1)
                                mm(ps[:, 4 + c2, :], mean_of[:, :], proj[:, 2 * c2:2 * c2 + 2, :],
                                   start=True, stop=True).then_inc(gn_var, 1)
                    pe.wait_ge(v_ready, BLOCKS)
                    pe.wait_ge(tile_out, 4 + BANKS + IN_GROUPS)
                    for hd in range(HEADS):
                        for b in range(BLOCKS):
                            o = ps[:, hd // 2, (hd % 2) * SEQ + b * P:(hd % 2) * SEQ + (b + 1) * P]
                            mm(o, ones_row[0:1, :], sgub[0:1, hd * P:(hd + 1) * P], start=True, stop=False)
                            last = mm(o, vt[:, b, hd * P:(hd + 1) * P], wmT[:, hd, :], start=False, stop=True)
                        if hd % 2:
                            last.then_inc(gated, 1)
                chunks = [first + c for first, _ in ROW_ORDER[L] for c in range(CH)]
                for n2, k in enumerate(chunks):
                    if n2 == 0:
                        if L == 0:
                            pe.wait_ge(y_split, len(WINDOWS))
                        else:
                            pe.wait_ge(sgu_out, CH // 2)
                            pe.wait_ge(gn_root, CH // 2)
                        pe.wait_ge(tile_out, 4 + BANKS * L + IN_GROUPS)
                    pe.wait_ge(y_split, CH * L + n2 // 2 + 1)
                    for half in range(2):
                        n = 2 * n2 + half
                        pe.wait_ge(low_done, RAW + L * PARTS + IN_GROUPS * QUARTERS + n + 1)
                        for b in range(BLOCKS):
                            bs = slice(b * P, (b + 1) * P)
                            for q in range(2):
                                cs = slice(q * BANK, (q + 1) * BANK)
                                last = three_passes(ps[:, 4 * b + 2 * half + q, :],
                                                    (zT_high[:, k, bs], zT_low[:, k, bs]),
                                                    (w_high[:, n % PAIRS, cs], w_low[:, n % PAIRS, cs]),
                                                    start=(n2 == 0), stop=(n2 == KD - 1))
                        last.then_inc(pair_free, 1)

                transposes(2 * L + 1)
                def score(b, t):
                    pe.wait_ge(tile_out, 4 + BANKS * L + IN_GROUPS + t + 1)
                    for hd in (2 * t, 2 * t + 1):
                        o = ps[:, 4 * (1 - b) + t, (hd % 2) * SEL:(hd % 2 + 1) * SEL]
                        last = mm(o, qT[:, hd, b * P:(b + 1) * P], subT[:, hd, :], start=True, stop=True)
                    last.then_inc(q_scored, 1)

                for t in range(4):
                    if t == 0:
                        pe.wait_ge(h_mixed, 8 * (L + 1))
                    pe.wait_ge(tile_out, BANKS * L + IN_GROUPS + t + 1)
                    channel_bank(t, RAW + L * PARTS + Q_AT + t * QUARTERS)
                    if t == 0:
                        score(0, 0)
                for t in range(1, 4):
                    score(0, t)
                for t in range(4):
                    score(1, t)
                for b in range(BLOCKS):
                    pe.wait_ge(scores_out, (L + 1) * BLOCKS * HEADS // 2)
                    for q in range(D // BANK):
                        mm(ps[:, 4 * b + q, :], ident[:, :], h[:, b, q * BANK:(q + 1) * BANK],
                           start=True, stop=False)
                    rows = (L * BLOCKS + b) * HEADS * TOPK
                    with pe.Fori(0, HEADS) as i:
                        for j in range(TOPK):
                            pe.wait_ge(diag_done, i * TOPK + (rows + j + 1))
                            per = TOPK // VSLOTS
                            pe.wait_ge(v_in[j % VSLOTS],
                                       i * (16 * per) + 16 * (rows // VSLOTS + j // VSLOTS + 1))
                            for q in range(D // BANK):
                                last = mm(ps[:, 4 * b + q, :], diag[:, j, :],
                                          vslot[j % VSLOTS][:, q * BANK:(q + 1) * BANK], start=False, stop=False)
                            last.then_inc(v_free, 1)
                    for q in range(D // BANK):
                        last = mm(ps[:, 4 * b + q, :], zeros[:, :],
                                  zeros[:, 0:1].to_broadcast([P, BANK]), start=False, stop=True)
                    last.then_inc(block_done, 1)

        @block.scalar
        def _(act):
            a = nc.scalar.activation

            def norm_start(m):
                for b in range(BLOCKS):
                    a(zn[:, b, :], h[:, b, :], ACT.Square, accum_out=square_sum[:, b:b + 1]).then_inc(squared, 1)
                act.wait_ge(squared, BLOCKS * (m + 1))
                a(root[:, :], square_sum[:, :], ACT.Sqrt, scale=1.0 / D, bias=eps_col[:, :]).then_inc(rooted, 1)

            def norm_rows(m, gain_at):
                act.wait_ge(rstd_ready, m + 1)
                a(zn[:, 1, :], h[:, 1, :], ACT.Copy, scale=rstd[:, 1:2]).then_inc(zn_ready, 1)
                for kk in range(KD // 2):
                    act.wait_ge(turned, (KD // 2) * m + kk + 1)
                    if kk == 0:
                        act.wait_ge(cols_ready, 3)
                    for k in (2 * kk, 2 * kk + 1):
                        last = a(zT_high[:, k, :], ps[:, kk % 4, (k % 2) * SEQ:(k % 2 + 1) * SEQ], ACT.Copy,
                                 scale=colA[:, gain_at + k:gain_at + k + 1])
                    last.then_inc(zT_rounded, 1)

            def high_group(L, group, odd, i=0):
                for q in range(QUARTERS):
                    slot = QUARTERS * odd + q
                    n = L * PARTS + group * QUARTERS + q
                    act.wait_ge(raw_in[slot], i * 16 + 16 * (n // RAW + 1))
                    act.wait_ge(pair_free, i * RAW + (n + 1))
                    a(w_high[:, q, :], raw[:, slot, :], ACT.Copy).then_inc(high_done, 1)

            def bank_out(t, out_, func, used):
                act.wait_ge(pair_free, used)
                a(out_, ps[:, t, :].rearrange("p (c t) -> p c t", c=2), func).then_inc(tile_out, 1)

            def v_and_group_squares():
                act.wait_ge(v_centred, BLOCKS)
                for b in range(BLOCKS):
                    a(padded[:, 4 * b:4 * b + 4, 0:SEQ], vt[:, b, :].rearrange("p (c t) -> p c t", c=4), ACT.Square,
                      accum_out=vstat[:, 1, b:b + 1]).then_inc(v_squared, 1)
                act.wait_ge(v_squared, BLOCKS)
                a(vstat[:, 2, :], vstat[:, 1, :], ACT.Sqrt, scale=1.0 / SECTION, bias=eps_col[:, :])\
                    .then_inc(v_root, 1)
                for c2 in range(CH // 2):
                    act.wait_ge(gn_centred, c2 + 1)
                    a(proj[:, 2 * c2:2 * c2 + 2, :], proj[:, CH + 2 * c2:CH + 2 * c2 + 2, :], ACT.Square)\
                        .then_inc(gn_squared, 1)

            def group_output():
                for c2 in range(CH // 2):
                    act.wait_ge(gn_var, c2 + 1)
                    a(proj[:, 2 * c2:2 * c2 + 2, :], ps[:, 4 + c2, :].rearrange("p (c t) -> p c t", c=2),
                      ACT.Sqrt, bias=eps_col[:, :]).then_inc(gn_root, 1)
                for c in range(CH):
                    act.wait_ge(gn_scaled, c // 2 + 1)
                    a(proj[:, CH + c, :], proj[:, CH + c, :], ACT.Silu,
                      scale=colA[:, ROWS_GNG + c:ROWS_GNG + c + 1],
                      bias=colA[:, ROWS_GNB + c:ROWS_GNB + c + 1]).then_inc(gn_out, 1)

            def group_rounded():
                for c2 in range(CH // 2):
                    act.wait_ge(gn_out, 2 * c2 + 2)
                    a(zT_high[:, CH + 2 * c2:CH + 2 * c2 + 2, :], proj[:, CH + 2 * c2:CH + 2 * c2 + 2, :],
                      ACT.Copy).then_inc(y_rounded, 1)

            act.wait_ge(made, CONSTANTS)
            act.wait_ge(params_turned, 1)
            a(colA[:, :], ps[:, 6, 0:ROWS_A], ACT.Copy).then_inc(cols_ready, 1)
            for s in range(2):
                a(convT[:, s * ROWS_B:(s + 1) * ROWS_B], ps[:, 6, (s + 1) * P:(s + 1) * P + ROWS_B], ACT.Copy)\
                    .then_inc(cols_ready, 1)
            act.wait_ge(x_in, 16 * BLOCKS)
            for L in range(LAYERS):
                norm_start(2 * L)
                high_group(L, 0, 0)
                norm_rows(2 * L, ROWS_MIX + KD * L)
                act.wait_ge(keys_turned, L + 1)
                for p2 in range(2):
                    rows = slice(64 * p2, 64 * p2 + 64)
                    a(subT[rows, :, p2 * NKEYS:(p2 + 1) * NKEYS],
                      ps[rows, 4:6, :].rearrange("p a (h n) -> p (a h) n", n=NKEYS), ACT.Copy).then_inc(keys_ready, 1)
                used = PAIRS + L * PARTS
                if L == 0:
                    with act.Fori(0, 4) as i:
                        for t in range(4):
                            odd = (t + 1) % 2
                            high_group(L, t + 1, odd, i * 2)
                            value = i * (4 * QUARTERS) + (used + (t + 1) * QUARTERS)
                            wait_unfused(act, (pair_free, value))
                            a(proj[:, bass.ds(i * CH + 2 * t, 2), :],
                              ps[:, t, :].rearrange("p (c t) -> p c t", c=2), ACT.Copy).then_inc(tile_out, 1)
                    for gr in range(len(WINDOWS)):
                        act.wait_ge(pool_mixed, gr + 1)
                        for dd in range(2):
                            c = 2 * gr + dd
                            last = a(zT_high[:, c, :], ps[:, 4 + gr, dd * SEQ:(dd + 1) * SEQ], ACT.Copy,
                                     scale=colA[:, ROWS_SCALE + c:ROWS_SCALE + c + 1])
                        last.then_inc(y_rounded, 1)
                    for c2 in range(CH // 2):
                        act.wait_ge(conv_out, c2 + 1)
                        a(zT_high[:, CH + 2 * c2:CH + 2 * c2 + 2, :], proj[:, CH + 2 * c2:CH + 2 * c2 + 2, :],
                          ACT.Copy).then_inc(y_rounded, 1)
                else:
                    act.wait_ge(sgu_turned, 1)
                    for s in range(2):
                        a(wmT[:, 4 * s:4 * s + 4, :], ps[:, 6 + s, :].rearrange("p (h t) -> p h t", h=4), ACT.Copy)\
                            .then_inc(sgu_copied, 1)
                    for group in range(IN_GROUPS):
                        high_group(L, group + 1, (group + 1) % 2)
                        done = used + (group + 1) * QUARTERS
                        t = group % 4
                        if group < 8:
                            at = (group % 2) * CH + 2 * (group // 2)
                            bank_out(t, proj[:, at:at + 2, :], (ACT.Copy, ACT.Sigmoid)[group % 2], done)
                        elif group < 12:
                            act.wait_ge(pair_free, done)
                            for b in range(BLOCKS):
                                last = a(vt[:, b, t * WCOLS:(t + 1) * WCOLS], ps[:, t, b * WCOLS:(b + 1) * WCOLS],
                                         ACT.Gelu, accum_out=vsum[:, b, t:t + 1])
                            last.then_inc(tile_out, 1)
                        else:
                            bank_out(t, proj[:, 2 * CH + 2 * t:2 * CH + 2 * t + 2, :], ACT.Gelu, done)
                        if group == 12:
                            v_and_group_squares()
                        if group == 14:
                            group_output()
                    group_rounded()
                    for c2 in range(CH // 2):
                        act.wait_ge(sgu_out, c2 + 1)
                        a(zT_high[:, 2 * c2:2 * c2 + 2, :], proj[:, 2 * CH + 2 * c2:2 * CH + 2 * c2 + 2, :], ACT.Copy)\
                            .then_inc(y_rounded, 1)

                for group in range(IN_GROUPS + 1, IN_GROUPS + OUT_GROUPS + 1):
                    high_group(L, group, group % 2)
                act.wait_ge(h_mixed, 8 * (L + 1))
                norm_start(2 * L + 1)
                norm_rows(2 * L + 1, ROWS_FFN + KD * L)
                def copy_scores(source):
                    a(sc, source, ACT.Copy).then_inc(head_in, 1)

                def exponentials(i, heads):
                    act.wait_ge(under_max, i + (heads + 1))
                    a(expo[:, :], below[:, :], ACT.Exp, accum_out=denom[:, 0:1]).then_inc(exp_done, 1)

                def weighting(i, b, heads):
                    act.wait_ge(u_free, i * TOPK + (L * SLOTS_FREED_U + USLOTS + (b * HEADS + 1) * TOPK))
                    a(gelu[:, :], dots[:, :], ACT.Gelu).then_inc(gelu_done, 1)
                    act.wait_ge(weights_done, i + (heads + 1))
                    act.wait_ge(v_free, i * TOPK + (L * SLOTS_FREED_V + VSLOTS + b * HEADS * TOPK))
                    for j in range(TOPK):
                        a(diag[:, j, :], ident[:, :], ACT.Copy, scale=weight[:, j:j + 1]).then_inc(diag_done, 1)

                for t in range(4):
                    group = IN_GROUPS + OUT_GROUPS + t
                    if t < 3:
                        high_group(L, group + 1, (group + 1) % 2)
                    bank_out(t, qT[:, 2 * t:2 * t + 2, :], ACT.Copy, used + (group + 1) * QUARTERS)
                    if t == 0:
                        act.wait_ge(q_scored, L * HEADS + 1)
                        act.wait_ge(experts_u, L * BLOCKS * HEADS + 1)
                        copy_scores(ps[:, 4, 0:SEL].rearrange("p (x n) -> p x n", x=2))
                    if t == 1:
                        exponentials(0, L * BLOCKS * HEADS)
                for b in range(BLOCKS):
                    for t in range(4):
                        act.wait_ge(q_scored, L * HEADS + b * 4 + t + 1)
                        a(scores[:, b, 2 * t:2 * t + 2, :],
                          ps[:, 4 * (1 - b) + t, :].rearrange("p (h n) -> p h n", h=2), ACT.Copy).then_inc(scores_out, 1)
                act.wait_ge(scores_out, (L + 1) * HEADS)
                a(freed[:, L:L + 1], eps_col[:, :], ACT.Copy).then_inc(v_free, VSLOTS)
                weighting(0, 0, L * BLOCKS * HEADS)
                for b in range(BLOCKS):
                    heads = (L * BLOCKS + b) * HEADS
                    with act.Fori(1 - b, HEADS) as i:
                        wait_unfused(act, (experts_u, i + (heads + 1)))
                        copy_scores(scores[:, b, bass.ds(i, 1), :].rearrange("p a (x n) -> p (a x) n", x=2))
                        exponentials(i, heads)
                        weighting(i, b, heads)
                for b in range(BLOCKS):
                    act.wait_ge(block_done, L * BLOCKS + b + 1)
                    a(h[:, b, :], ps[:, 4 * b:4 * b + 4, :].rearrange("p a n -> p (a n)"), ACT.Copy)\
                        .then_inc(h_expert, 1)
                act.wait_ge(h_expert, BLOCKS * (L + 1))
            norm_start(2 * LAYERS)

        @block.vector
        def _(dve):
            v = nc.vector
            steps = [0]

            def step(ins):
                steps[0] += 1
                ins.then_inc(dve_step, 1)
                dve.wait_ge(dve_step, steps[0])

            def norm_scale(m):
                dve.wait_ge(rooted, m + 1)
                v.reciprocal(rstd[:, :], root[:, :]).then_inc(rstd_ready, 1)
                dve.wait_ge(rstd_ready, m + 1)

            def norm_rows(m, gain_at):
                norm_scale(m)
                v.tensor_scalar(zn[:, 0, :], h[:, 0, :], rstd[:, 0:1], None, ALU.mult).then_inc(zn_ready, 1)
                if m == 0:
                    dve.wait_ge(cols_ready, 3)
                for kk in range(KD // 2):
                    dve.wait_ge(zT_rounded, (KD // 2) * m + kk + 1)
                    for k in (2 * kk, 2 * kk + 1):
                        last = v.scalar_tensor_tensor(zT_low[:, k, :], ps[:, kk % 4, (k % 2) * SEQ:(k % 2 + 1) * SEQ],
                                                      colA[:, gain_at + k:gain_at + k + 1],
                                                      zT_high[:, k, :].bitcast(F32), ALU.mult, ALU.subtract)
                    last.then_inc(zT_split, 1)

            def split_y(n, at, exact):
                dve.wait_ge(y_rounded, n + 1)
                v.tensor_tensor(zT_low[:, at:at + 2, :], exact, zT_high[:, at:at + 2, :].bitcast(F32),
                                ALU.subtract).then_inc(y_split, 1)

            v.memset(token[:, 0:1], 0.0).then_inc(low_done, RAW)
            v.memset(token[:, 1:2], 0.0).then_inc(tile_out, 4)
            v.memset(token[:, 2:3], 0.0).then_inc(pair_free, PAIRS)
            v.memset(token[:, 3:4], 0.0).then_inc(experts_u, 1)
            dve.wait_ge(made, CONSTANTS)

            for L in range(LAYERS):
                norm_rows(2 * L, ROWS_MIX + KD * L)
                if L == 0:
                    dve.wait_ge(keys_turned, 1)
                    step(v.memset(padpool[:, :, :, 0:WINDOWS[-1]], 0.0))
                    for gr, window in enumerate(WINDOWS):
                        step(v.tensor_scalar(inv_count[:, :], position[:, :], float(window), None, ALU.min))
                        step(v.reciprocal(inv_count[:, :], inv_count[:, :]))
                        dve.wait_ge(tile_out, 4 + gr + 1)
                        own = proj[:, 2 * gr:2 * gr + 2, :]
                        W0 = WINDOWS[-1]
                        step(v.tensor_copy(padpool[:, 0, :, W0:], own))
                        lag, at = 1, 0
                        while lag < window:
                            step(v.tensor_tensor(padpool[:, 1 - at, :, W0:], padpool[:, at, :, W0:],
                                                 padpool[:, at, :, W0 - lag:W0 - lag + SEQ], ALU.add))
                            lag, at = 2 * lag, 1 - at
                        step(v.tensor_tensor(padpool[:, at, :, W0:], padpool[:, at, :, W0:],
                                             inv_count[:, None, :].to_broadcast([P, 2, SEQ]), ALU.mult))
                        v.tensor_tensor(own, padpool[:, at, :, W0:], own, ALU.subtract).then_inc(pooled, 1)
                    dve.wait_ge(pooled, len(WINDOWS))
                    edge = SHORT - 1
                    step(v.memset(padshort[:, :, 0:edge], 0.0))
                    for t in range(4):
                        dve.wait_ge(tile_out, 4 + 12 + t + 1)
                        cs = slice(2 * t, 2 * t + 2)
                        step(v.tensor_tensor(padshort[:, cs, edge:], proj[:, 2 * CH + 2 * t:2 * CH + 2 * t + 2, :],
                                             proj[:, 3 * CH + 2 * t:3 * CH + 2 * t + 2, :], ALU.mult))
                        tap = lambda k, c: colA[:, ROWS_SHORT + k * CH + c:ROWS_SHORT + k * CH + c + 1]
                        acc = lambda c: proj[:, 2 * CH + c, :]
                        for c in (2 * t, 2 * t + 1):
                            step(v.tensor_scalar(acc(c), padshort[:, c, 0:SEQ], tap(0, c), None, ALU.mult))
                        for k in range(1, SHORT):
                            for c in (2 * t, 2 * t + 1):
                                step(v.scalar_tensor_tensor(acc(c), padshort[:, c, k:k + SEQ], tap(k, c), acc(c),
                                                            ALU.mult, ALU.add))
                        v.tensor_tensor(proj[:, CH + 2 * t:CH + 2 * t + 2, :], proj[:, CH + 2 * t:CH + 2 * t + 2, :],
                                        proj[:, 2 * CH + 2 * t:2 * CH + 2 * t + 2, :], ALU.mult).then_inc(conv_out, 1)
                    for gr in range(len(WINDOWS)):
                        dve.wait_ge(y_rounded, gr + 1)
                        for dd in range(2):
                            c = 2 * gr + dd
                            last = v.scalar_tensor_tensor(zT_low[:, c, :], ps[:, 4 + gr, dd * SEQ:(dd + 1) * SEQ],
                                                          colA[:, ROWS_SCALE + c:ROWS_SCALE + c + 1],
                                                          zT_high[:, c, :].bitcast(F32), ALU.mult, ALU.subtract)
                        last.then_inc(y_split, 1)
                    for c2 in range(CH // 2):
                        split_y(4 + c2, CH + 2 * c2, proj[:, CH + 2 * c2:CH + 2 * c2 + 2, :])
                else:
                    TB = 4 + BANKS * L
                    edge = TAPS - 1
                    dve.wait_ge(keys_turned, 2)
                    dve.wait_ge(sgu_turned, 1)
                    step(v.memset(padded[:, :, 0:edge], 0.0))
                    for t in range(4):
                        dve.wait_ge(tile_out, TB + 2 * t + 2)
                        cs = slice(2 * t, 2 * t + 2)
                        step(v.tensor_tensor(padded[:, cs, edge:], proj[:, cs, :],
                                             proj[:, CH + 2 * t:CH + 2 * t + 2, :], ALU.mult))
                        before = t * TAPS * 2
                        for c in (2 * t, 2 * t + 1):
                            v.tensor_scalar(proj[:, c, :], padded[:, c, 0:SEQ], convT[:, c:c + 1],
                                            colA[:, ROWS_CONVB + c:ROWS_CONVB + c + 1], ALU.mult, ALU.add)\
                                .then_inc(conv_step, 1)
                        with dve.Fori(1, TAPS) as k:
                            for c in (2 * t, 2 * t + 1):
                                dve.wait_ge(conv_step, k * 2 + (before + c % 2 - 1))
                                v.scalar_tensor_tensor(proj[:, c, :], padded[:, c, bass.ds(k, SEQ)],
                                                       convT[:, bass.ds(k * CH + c, 1)], proj[:, c, :],
                                                       ALU.mult, ALU.add).then_inc(conv_step, 1)
                    dve.wait_ge(tile_out, TB + 12)
                    dve.wait_ge(shared_in, 48)
                    step(v.tensor_reduce(vstat[:, 0, :], vsum[:, :, :], AX.X, ALU.add))
                    step(v.tensor_scalar(vstat[:, 0, :], vstat[:, 0, :], 1.0 / SECTION, None, ALU.mult))
                    for b in range(BLOCKS):
                        v.tensor_scalar(vt[:, b, :], vt[:, b, :], vstat[:, 0, b:b + 1], None, ALU.subtract)\
                            .then_inc(v_centred, 1)
                    dve.wait_ge(v_root, 1)
                    step(v.reciprocal(vstat[:, 3, :], vstat[:, 2, :]))
                    for b in range(BLOCKS):
                        step(v.scalar_tensor_tensor(vt[:, b, :], vt[:, b, :], vstat[:, 3, b:b + 1], vgb[:, 0, :],
                                                    ALU.mult, ALU.mult))
                        v.tensor_tensor(vt[:, b, :], vt[:, b, :], vgb[:, 1, :], ALU.add).then_inc(v_ready, 1)
                    for c2 in range(CH // 2):
                        cs = slice(2 * c2, 2 * c2 + 2)
                        dve.wait_ge(gn_mean, c2 + 1)
                        v.tensor_tensor(proj[:, CH + 2 * c2:CH + 2 * c2 + 2, :], proj[:, cs, :],
                                        ps[:, 4 + c2, :].rearrange("p (c t) -> p c t", c=2), ALU.subtract)\
                            .then_inc(gn_centred, 1)
                    for c2 in range(CH // 2):
                        cs = slice(2 * c2, 2 * c2 + 2)
                        zs = slice(CH + 2 * c2, CH + 2 * c2 + 2)
                        dve.wait_ge(gn_root, c2 + 1)
                        step(v.reciprocal(proj[:, cs, :], proj[:, cs, :]))
                        v.tensor_tensor(proj[:, zs, :], proj[:, zs, :], proj[:, cs, :], ALU.mult)\
                            .then_inc(gn_scaled, 1)
                    for c2 in range(CH // 2):
                        split_y(CH + c2, CH + 2 * c2, proj[:, CH + 2 * c2:CH + 2 * c2 + 2, :])
                    for c2 in range(CH // 2):
                        dve.wait_ge(gated, c2 + 1)
                        v.tensor_tensor(proj[:, 2 * CH + 2 * c2:2 * CH + 2 * c2 + 2, :],
                                        proj[:, 2 * CH + 2 * c2:2 * CH + 2 * c2 + 2, :],
                                        ps[:, c2, :].rearrange("p (c t) -> p c t", c=2), ALU.mult)\
                            .then_inc(sgu_out, 1)
                    for c2 in range(CH // 2):
                        split_y(CH + 4 + c2, 2 * c2, proj[:, 2 * CH + 2 * c2:2 * CH + 2 * c2 + 2, :])

                dve.wait_ge(pair_free, PAIRS + L * PARTS + Q_AT)
                for b in range(BLOCKS):
                    for q in range(D // BANK):
                        s = slice(q * BANK, (q + 1) * BANK)
                        v.tensor_tensor(h[:, b, s], ps[:, 4 * b + q, :], h[:, b, s], ALU.add).then_inc(h_mixed, 1)
                norm_rows(2 * L + 1, ROWS_FFN + KD * L)
                dve.wait_ge(gain_in, 16 * (L + 1))
                for b in range(BLOCKS):
                    v.tensor_tensor(zn[:, b, :], zn[:, b, :], gB[:, :], ALU.mult).then_inc(xn_ready, 1)

                dve.wait_ge(xn_ready, BLOCKS * (L + 1))
                v.memset(token[:, 4 + L:5 + L], 0.0).then_inc(u_free, USLOTS)
                for b in range(BLOCKS):
                    heads = (L * BLOCKS + b) * HEADS
                    with dve.Fori(0, HEADS) as i:
                        n = [0]

                        def routed(ins, unfused=False):
                            n[0] += 1
                            ins.then_inc(route_step, 1)
                            value = i * ROUTE_STEPS + (heads * ROUTE_STEPS + n[0])
                            if unfused:
                                wait_unfused(dve, (route_step, value))
                            else:
                                dve.wait_ge(route_step, value)

                        def top16(values, spare, best_, besti_):
                            routed(v.max(best_[0], values), True)
                            routed(v.max_index(besti_[0], best_[0], values), True)
                            routed(v.match_replace(spare, best_[0], values, LOWEST), True)
                            routed(v.max(best_[1], spare), True)
                            routed(v.max_index(besti_[1], best_[1], spare), True)

                        wait_unfused(dve, (head_in, i + (heads + 1)))
                        for p2 in range(2):
                            halves = [slice(0, 8), slice(8, 16)]
                            top16(sc[:, p2, :], sc2[:, p2, :], [top[:, p2, x] for x in halves],
                                  [topi[:, p2, x] for x in halves])
                        routed(v.tensor_scalar(topf[:, 0, :], topi[:, 0, :], float(NKEYS * L), None, ALU.add))
                        routed(v.tensor_copy(topf[:, 1, :], topi[:, 1, :]))
                        routed(v.tensor_tensor(cand[:, :, :], top[:, 0, :, None].to_broadcast([P, TOPK, TOPK]),
                                               top[:, 1, None, :].to_broadcast([P, TOPK, TOPK]), ALU.add), True)
                        flat = cand[:, :, :].rearrange("p a b -> p (a b)")
                        top16(flat, cand2[:, :], [best[:, x] for x in halves], [besti[:, x] for x in halves])
                        v.tensor_scalar(below[:, :], best[:, :], best[:, 0:1], None, ALU.subtract)\
                            .then_inc(under_max, 1)
                        routed(v.tensor_scalar(pos[:, 0, :], besti[:, :], 4, None, ALU.logical_shift_right))
                        routed(v.tensor_scalar(pos[:, 1, :], besti[:, :], TOPK - 1, None, ALU.bitwise_and))
                        for p2 in range(2):
                            o = onehot[:, p2, :, :]
                            routed(v.tensor_tensor(o, pos[:, p2, :, None].to_broadcast([P, TOPK, TOPK]),
                                                   iota16[:, None, :].to_broadcast([P, TOPK, TOPK]), ALU.is_equal))
                            routed(v.tensor_tensor(o, o, topf[:, p2, None, :].to_broadcast([P, TOPK, TOPK]),
                                                   ALU.mult))
                            routed(v.tensor_reduce(key[:, p2, :], o, AX.X, ALU.add))
                        v.scalar_tensor_tensor(expert_u[:, :], key[:, 0, :], float(NKEYS), key[:, 1, :],
                                               ALU.mult, ALU.add).then_inc(experts_u, 1)
                        for j in range(TOPK):
                            slot = uslot[j % USLOTS]
                            per = TOPK // USLOTS
                            dve.wait_ge(u_in[j % USLOTS],
                                        i * (16 * per) + 16 * (heads * per + j // USLOTS + 1))
                            v.tensor_tensor_reduce(out=slot, in0=slot, in1=zn[:, b, :], scale=1.0, scalar=0.0,
                                                   op0=ALU.mult, op1=ALU.add,
                                                   accum_out=dots[:, j:j + 1]).then_inc(u_free, 1)
                            if j == TOPK // 2 - 1:
                                dve.wait_ge(exp_done, i + (heads + 1))
                                routed(v.reciprocal(denom[:, 1:2], denom[:, 0:1]))
                                v.tensor_scalar(gates[:, :], expo[:, :], denom[:, 1:2], None, ALU.mult)\
                                    .then_inc(route_step, 1)
                                n[0] += 1
                                dve.wait_ge(v_free, i * TOPK + (L * SLOTS_FREED_V + VSLOTS + b * HEADS * TOPK))
                                v.scalar_tensor_tensor(expert_v[:, :], key[:, 0, :], float(NKEYS), key[:, 1, :],
                                                       ALU.mult, ALU.add).then_inc(experts_v, 1)
                        assert n[0] == ROUTE_STEPS, n
                        dve.wait_ge(gelu_done, i + (heads + 1))
                        dve.wait_ge(route_step, i * ROUTE_STEPS + (heads + 1) * ROUTE_STEPS)
                        v.tensor_tensor(weight[:, :], gelu[:, :], gates[:, :], ALU.mult).then_inc(weights_done, 1)

            norm_scale(2 * LAYERS)
            dve.wait_ge(gain_in, 16 * (LAYERS + 1))
            for b in range(BLOCKS):
                v.scalar_tensor_tensor(zn[:, b, :], h[:, b, :], rstd[:, b:b + 1], gB[:, :],
                                       ALU.mult, ALU.mult).then_inc(result_ready, 1)


ROUTE_STEPS = 28

_INS = ['x', 'mix_norm_g', 'ffn_norm_g', 'ev_w_in', 'ev_pool_w', 'ev_pool_scale', 'ev_conv_w', 'ev_w_out',
        'od_w_in', 'od_v_norm_g', 'od_v_norm_b', 'od_sgu_w', 'od_sgu_b', 'od_conv_w', 'od_conv_b',
        'od_gn_g', 'od_gn_b', 'od_w_out', 'peer_w_q', 'peer_subkeys', 'peer_u', 'peer_v', 'final_norm_g']


def kernel(**inputs):
    import numpy as np
    import concourse.bacc as bacc
    from concourse import mybir as mb
    from concourse.bass_utils import run_bass_kernel_spmd as run

    nc = bacc.Bacc("TRN2", target_bir_lowering=False, num_devices=1)
    arrays, args = {}, []
    for name in _INS:
        a = np.ascontiguousarray(inputs[name])
        arrays[f"in_{name}"] = a
        args.append(nc.dram_tensor(f"in_{name}", a.shape, mb.dt.from_np(a.dtype), kind="ExternalInput").ap())
    args.append(nc.dram_tensor("out", (1, SEQ, D), mb.dt.float32, kind="ExternalOutput").ap())
    two_layers(nc, *args)
    return run(nc, [arrays], core_ids=[0]).results[0]["out"]
```

```python
from contextlib import ExitStack

import concourse.bass as bass
from concourse import mybir

F32 = mybir.dt.float32
F32R = mybir.dt.float32r
I32 = mybir.dt.int32
U32 = mybir.dt.uint32
ALU = mybir.AluOpType
ACT = mybir.ActivationFunctionType
AX = mybir.AxisListType

P = 128
D = 2048
SEQ = 256
BLOCKS = SEQ // P
KD = D // P
LAYERS = 2
BANK = 512
WCOLS = 256
SECTION = 4 * WCOLS
CH = SECTION // P
PART = 1024
QUARTERS = 4
RAW = 8
PAIRS = 4
IN_GROUPS, OUT_GROUPS, Q_GROUPS = 16, 8, 4
GROUPS = IN_GROUPS + OUT_GROUPS + Q_GROUPS
PARTS = GROUPS * QUARTERS
BANKS = IN_GROUPS + Q_GROUPS
WINDOWS = (2, 4, 8, 16)
SHORT = 3
TAPS = 31
HEADS = 8
TOPK = 16
NKEYS = 128
SEL = 2 * NKEYS
USLOTS, VSLOTS = 4, 8
DVE_ROWS = (9, 11, 13, 15)
EPS = 1e-6
LOWEST = -3.0e38

ROWS_MIX, ROWS_FFN, ROWS_SCALE, ROWS_SHORT = 0, 32, 64, 72
ROWS_CONVB, ROWS_GNG, ROWS_GNB, ROWS_A = 96, 104, 112, 120
ROWS_B = TAPS * CH // 2


def two_layers(nc, x, mix_norm_g, ffn_norm_g, ev_w_in, ev_pool_w, ev_pool_scale, ev_conv_w, ev_w_out,
               od_w_in, od_v_norm_g, od_v_norm_b, od_sgu_w, od_sgu_b, od_conv_w, od_conv_b,
               od_gn_g, od_gn_b, od_w_out, peer_w_q, peer_subkeys, peer_u, peer_v, final_norm_g, out):
    w_in = (ev_w_in[0], od_w_in[0])
    w_out = (ev_w_out[0], od_w_out[0])
    by_rows = lambda w: w.rearrange("(k p) c -> p k c", p=P)
    chunked = lambda v: v.rearrange("(r c) -> r c", c=P)

    with ExitStack() as ctx:
        sb = lambda name, shape, dt=F32: ctx.enter_context(nc.sbuf_tensor(name, shape, dt))
        sem = lambda name: ctx.enter_context(nc.semaphore(name))

        h = sb("h", [P, BLOCKS, D])
        xn = sb("xn", [P, BLOCKS, D])
        scale = [xn[:, b, 0:P] for b in range(BLOCKS)]
        with ExitStack() as early:
            esb = lambda name, shape, dt=F32: early.enter_context(nc.sbuf_tensor(name, shape, dt))
            raw = esb("raw", [P, RAW, PART])
            w_high = esb("w_high", [P, PAIRS, PART], F32R)
            w_low = esb("w_low", [P, PAIRS, PART], F32R)
        vring = sb("vring", [P, VSLOTS, D])
        qT = sb("qT", [P, CH, SEQ])
        proj = sb("proj", [P, 4 * CH, SEQ])
        vt = proj[:, 3 * CH:4 * CH, :].rearrange("p k t -> p (k t)").rearrange("p (b c) -> p b c", b=BLOCKS)
        uring = proj[:, :, :].rearrange("p (s k) t -> p s (k t)", s=USLOTS)
        with ExitStack() as early:
            zT_high = early.enter_context(nc.sbuf_tensor("zT_high", [P, KD, SEQ], F32R))
        scores = sb("scores", [P, BLOCKS, HEADS, SEL])
        zT_low = sb("zT_low", [P, KD, SEQ], F32R)
        paramrow = proj[:, 0:2, :].rearrange("p k t -> p (k t)")[:, 0:3 * P].rearrange("p (a c) -> p a c", a=3)
        uslot = [uring[:, k, :] for k in range(USLOTS)]
        vslot = [vring[:, k, :] for k in range(VSLOTS)]
        gB = sb("gB", [P, D])
        sgub = gB[0:1, 0:HEADS * P]
        wmT = gB[:, HEADS * P:2 * HEADS * P].rearrange("p (h t) -> p h t", h=HEADS)
        inv_count, position = gB[:, 0:SEQ], gB[:, SEQ:2 * SEQ]
        shared = sb("shared", [P, 2 * SECTION])
        poolw = shared[:, :].rearrange("p (k d) -> p k d", d=WCOLS)
        vgb = shared[:, :].rearrange("p (a c) -> p a c", a=2)
        subT = sb("subT", [P, HEADS, SEL])
        scratch = sb("scratch", [P, CH * (SEQ + TAPS - 1)])
        subraw = scratch[:, 0:HEADS * P].rearrange("p (h k) -> p h k", h=HEADS)
        sguraw = scratch[:, HEADS * P:2 * HEADS * P].rearrange("p (h s) -> p h s", h=HEADS)
        padded = scratch[:, :].rearrange("p (c t) -> p c t", c=CH)
        SP_ = SEQ + SHORT - 1
        padshort = scratch[:, 0:CH * SP_].rearrange("p (c t) -> p c t", c=CH)
        WP = SEQ + WINDOWS[-1]
        padpool = scratch[:, 0:4 * WP].rearrange("p (a c t) -> p a c t", a=2, c=2)
        diag = scratch[:, 0:TOPK * P].rearrange("p (j c) -> p j c", c=P)
        ident = sb("ident", [P, P])
        mean_of = sb("mean_of", [P, P])
        ones_row = sb("ones_row", [1, P])
        zeros = sb("zeros", [P, P], mybir.dt.bfloat16)
        eps_col = sb("eps_col", [P, 1])
        colA = sb("colA", [P, ROWS_A])
        convT = sb("convT", [P, TAPS * CH])
        iota16 = sb("iota16", [P, TOPK])
        square_sum = sb("square_sum", [P, BLOCKS])
        root = sb("root", [P, BLOCKS])
        rstd = sb("rstd", [P, BLOCKS])
        vsum = sb("vsum", [P, BLOCKS, 4])
        vstat = sb("vstat", [P, 4, BLOCKS])
        grid = lambda at, a: shared[:, at:at + a * SEL]
        sc = grid(0, 1).rearrange("p (x n) -> p x n", x=2)
        sc2 = grid(SEL, 1).rearrange("p (x n) -> p x n", x=2)
        cand = grid(2 * SEL, 1).rearrange("p (a b) -> p a b", a=TOPK)
        cand2 = grid(3 * SEL, 1)
        onehot = grid(4 * SEL, 2).rearrange("p (x a b) -> p x a b", x=2, a=TOPK)
        top = sb("top", [P, 2, TOPK])
        topi = sb("topi", [P, 2, TOPK], U32)
        topf = sb("topf", [P, 2, TOPK])
        best = sb("best", [P, TOPK])
        besti = sb("besti", [P, TOPK], U32)
        pos = sb("pos", [P, 2, TOPK], U32)
        key = sb("key", [P, 2, TOPK])
        below = sb("below", [P, TOPK])
        expo = sb("expo", [P, TOPK])
        denom = sb("denom", [P, 2])
        gates = sb("gates", [P, TOPK])
        expert_u = sb("expert_u", [P, TOPK], I32)
        expert_v = sb("expert_v", [P, TOPK], I32)
        dots = sb("dots", [P, TOPK])
        gelu = sb("gelu", [P, TOPK])
        weight = sb("weight", [P, TOPK])
        token = sb("token", [P, 4 + LAYERS])
        freed_by_act = sb("freed_by_act", [P, LAYERS])
        table = sb("table", [P, 1])
        ps = ctx.enter_context(nc.psum_tensor("ps", [P, 8, BANK], F32))

        made = sem("made")
        x_in = sem("x_in")
        rows_in = sem("rows_in")
        gain_in = sem("gain_in")
        shared_in = sem("shared_in")
        keys_in = sem("keys_in")
        sgu_in = sem("sgu_in")
        raw_in = [sem(f"raw_in{s}") for s in range(RAW)]
        high_done = sem("high_done")
        low_done = sem("low_done")
        pair_free = sem("pair_free")
        squared = sem("squared")
        rooted = sem("rooted")
        table_used = sem("table_used")
        rstd_ready = sem("rstd_ready")
        scale_ready = sem("scale_ready")
        turned = sem("turned")
        zT_rounded = sem("zT_rounded")
        zT_split = sem("zT_split")
        xn_ready = sem("xn_ready")
        params_turned = sem("params_turned")
        cols_ready = sem("cols_ready")
        keys_turned = sem("keys_turned")
        keys_ready = sem("keys_ready")
        sgu_turned = sem("sgu_turned")
        sgu_copied = sem("sgu_copied")
        sgu_masked = sem("sgu_masked")
        tile_out = sem("tile_out")
        pooled = sem("pooled")
        pool_mixed = sem("pool_mixed")
        conv_out = sem("conv_out")
        y_rounded = sem("y_rounded")
        y_split = sem("y_split")
        conv_step = sem("conv_step")
        conv_summed = sem("conv_summed")
        v_squared = sem("v_squared")
        v_centred = sem("v_centred")
        v_root = sem("v_root")
        v_ready = sem("v_ready")
        gn_mean = sem("gn_mean")
        gn_centred = sem("gn_centred")
        gn_squared = sem("gn_squared")
        gn_var = sem("gn_var")
        gn_root = sem("gn_root")
        gn_scaled = sem("gn_scaled")
        gn_out = sem("gn_out")
        gated = sem("gated")
        sgu_out = sem("sgu_out")
        h_mixed = sem("h_mixed")
        first_query = sem("first_query")
        first_copied = sem("first_copied")
        first_scored = sem("first_scored")
        q_scored = sem("q_scored")
        scores_out = sem("scores_out")
        head_in = sem("head_in")
        under_max = sem("under_max")
        exp_done = sem("exp_done")
        experts_u = sem("experts_u")
        experts_v = sem("experts_v")
        u_in = [sem(f"u_in{s}") for s in range(USLOTS)]
        v_in = [sem(f"v_in{s}") for s in range(VSLOTS)]
        u_free = sem("u_free")
        v_free = sem("v_free")
        v_summed = sem("v_summed")
        gelu_done = sem("gelu_done")
        weights_done = sem("weights_done")
        diag_done = sem("diag_done")
        block_done = sem("block_done")
        h_expert = sem("h_expert")
        result_ready = sem("result_ready")
        stored = sem("stored")
        dve_step = sem("dve_step")
        route_step = sem("route_step")

        SLOTS_FREED_U = USLOTS + BLOCKS * HEADS * TOPK
        SLOTS_FREED_V = VSLOTS + BLOCKS * HEADS * TOPK - len(DVE_ROWS)
        CONSTANTS = 9
        Q_AT = PARTS - Q_GROUPS * QUARTERS

        ROW_ORDER = (((0, 0), (CH, CH)), ((CH, 0), (0, CH)))

        block = ctx.enter_context(nc.Block())

        def wait_unfused(eng, *waits):
            if all(isinstance(value, int) for _, value in waits):
                for s, value in waits:
                    eng.wait_ge(s, value)
                return
            for _, value in waits:
                eng.to_reg(value)
            eng.wait_ge(made, CONSTANTS)
            for s, value in waits:
                eng.wait_ge(s, value)

        @block.sync
        def _(sp):
            for b in range(BLOCKS):
                sp.dma_start(h[:, b, :], x[0, b * P:(b + 1) * P, :]).then_inc(x_in, 16)
            rows = paramrow
            sp.dma_start(rows[ROWS_MIX:ROWS_MIX + 32, 0, :],
                         mix_norm_g.rearrange("l (k c) -> (l k) c", c=P)).then_inc(rows_in, 16)
            sp.dma_start(rows[ROWS_FFN:ROWS_FFN + 32, 0, :],
                         ffn_norm_g.rearrange("l (k c) -> (l k) c", c=P)).then_inc(rows_in, 16)
            sp.dma_start(rows[ROWS_SCALE:ROWS_SCALE + CH, 0, :], chunked(ev_pool_scale[0])).then_inc(rows_in, 16)
            sp.dma_start(rows[ROWS_SHORT:ROWS_SHORT + SHORT * CH, 0, :],
                         ev_conv_w[0].rearrange("k (r c) -> (k r) c", c=P)).then_inc(rows_in, 16)
            sp.dma_start(rows[ROWS_CONVB:ROWS_CONVB + CH, 0, :], chunked(od_conv_b[0])).then_inc(rows_in, 16)
            sp.dma_start(rows[ROWS_GNG:ROWS_GNG + CH, 0, :], chunked(od_gn_g[0])).then_inc(rows_in, 16)
            sp.dma_start(rows[ROWS_GNB:ROWS_GNB + CH, 0, :], chunked(od_gn_b[0])).then_inc(rows_in, 16)
            taps = od_conv_w[0].rearrange("k (r c) -> (k r) c", c=P)
            sp.dma_start(rows[0:ROWS_B, 1, :], taps[0:ROWS_B, :]).then_inc(rows_in, 16)
            sp.dma_start(rows[0:ROWS_B, 2, :], taps[ROWS_B:2 * ROWS_B, :]).then_inc(rows_in, 16)

            def load_part(slot, n, src):
                sp.wait_ge(low_done, n + 1)
                sp.dma_start(raw[:, slot, :].rearrange("p (k c) -> p k c", c=src.shape[-1]), src)\
                  .then_inc(raw_in[slot], 16)

            for L in range(LAYERS):
                win, wout, wq = by_rows(w_in[L]), by_rows(w_out[L]), by_rows(peer_w_q[L])

                def load_small():
                    if L:
                        sp.wait_ge(v_free, L * SLOTS_FREED_V)
                        sp.wait_ge(v_summed, L * len(DVE_ROWS))
                        sp.wait_ge(diag_done, L * BLOCKS * HEADS * TOPK)
                    sp.dma_start(subraw.rearrange("n h (p k) -> n h p k", p=2),
                                 peer_subkeys[L].rearrange("h p n k -> n h p k")).then_inc(keys_in, 16)
                    if L == 0:
                        sp.dma_start(poolw, ev_pool_w[0].rearrange("g (k p) d -> p (g k) d", p=P))\
                          .then_inc(shared_in, 16)
                    else:
                        sp.dma_start(sguraw, od_sgu_w[0].rearrange("h t s -> t h s")).then_inc(sgu_in, 16)
                        sp.dma_start(sgub, od_sgu_b[0:1].rearrange("o h t -> o (h t)")).then_inc(sgu_in, 16)
                        sp.dma_start(vgb[:, 0, :], od_v_norm_g[0:1, :].to_broadcast([P, SECTION]))\
                          .then_inc(shared_in, 16)
                        sp.dma_start(vgb[:, 1, :], od_v_norm_b[0:1, :].to_broadcast([P, SECTION]))\
                          .then_inc(shared_in, 16)

                GQ = 4 * QUARTERS
                if L == 0:
                    for m in range(GQ):
                        t, q = divmod(m, QUARTERS)
                        load_part(m % RAW, m, win[:, 4 * q:4 * q + 4, t * WCOLS:(t + 1) * WCOLS])
                        if m == RAW - 1:
                            load_small()
                    with sp.Fori(1, 4) as i:
                        for m in range(GQ):
                            t, q = divmod(m, QUARTERS)
                            load_part(m % RAW, i * GQ + m,
                                      win[:, 4 * q:4 * q + 4, bass.ds(i * SECTION + t * WCOLS, WCOLS)])
                else:
                    order = [(2 + t % 2, t // 2) for t in range(8)]
                    order += [(part, t) for part in (1, 0) for t in range(4)]
                    for m in range(IN_GROUPS * QUARTERS):
                        group, q = divmod(m, QUARTERS)
                        part, t = order[group]
                        at = part * SECTION + t * WCOLS
                        if m < RAW:
                            row = TOPK - VSLOTS + m * PART // D
                            if row in DVE_ROWS:
                                sp.wait_ge(v_summed, (L - 1) * len(DVE_ROWS) + DVE_ROWS.index(row) + 1)
                            else:
                                after = [j for j in range(row + 1, TOPK) if j not in DVE_ROWS]
                                sp.wait_ge(v_free, L * SLOTS_FREED_V - len(after))
                        load_part(m % RAW, L * PARTS + m, win[:, 4 * q:4 * q + 4, at:at + WCOLS])
                        if m == RAW - 1:
                            load_small()
                for first, n in ROW_ORDER[L]:
                    with sp.Fori(0, CH // (RAW // 2)) as i:
                        for m in range(RAW):
                            load_part(m, i * RAW + (L * PARTS + IN_GROUPS * QUARTERS + 2 * n + m),
                                      wout[:, bass.ds(i * (RAW // 2) + (first + m // 2), 1),
                                           (m % 2) * PART:(m % 2 + 1) * PART])
                    if n == 0:
                        if L:
                            sp.wait_ge(sgu_out, CH // 2)
                        else:
                            sp.wait_ge(pooled, len(WINDOWS))
                        sp.dma_start(gB[:, :], ffn_norm_g[L:L + 1, :].to_broadcast([P, D])).then_inc(gain_in, 16)
                for m in range(Q_GROUPS * QUARTERS):
                    t, q = divmod(m, QUARTERS)
                    load_part(m % RAW, L * PARTS + Q_AT + m, wq[:, 4 * q:4 * q + 4, t * WCOLS:(t + 1) * WCOLS])
            sp.wait_ge(xn_ready, BLOCKS * LAYERS)
            sp.dma_start(gB[:, :], final_norm_g.rearrange("(a c) -> a c", a=1).to_broadcast([P, D]))\
              .then_inc(gain_in, 16)
            for b in range(BLOCKS):
                for half in range(2):
                    s = slice(half * D // 2, (half + 1) * D // 2)
                    sp.wait_ge(result_ready, 2 * b + half + 1)
                    sp.dma_start(out[0, b * P:(b + 1) * P, s], xn[:, b, s]).then_inc(stored, 16)
            sp.wait_ge(stored, 16 * 2 * BLOCKS)

        @block.gpsimd
        def _(pool):
            g = nc.gpsimd
            g.memset(ident[:, :], 0.0).then_inc(made, 1)
            g.memset(mean_of[:, :], 1.0 / P).then_inc(made, 1)
            g.memset(ones_row[:, :], 1.0).then_inc(made, 1)
            g.memset(zeros[:, :], 0.0).then_inc(made, 1)
            g.memset(eps_col[:, :], EPS).then_inc(made, 1)
            g.memset(subT[:, :, :], 0.0).then_inc(made, 1)
            g.iota(position[:, :], pattern=[[1, SEQ]], base=1, channel_multiplier=0,
                   allow_small_or_imprecise_dtypes=True).then_inc(made, 1)
            g.iota(iota16[:, :], pattern=[[1, TOPK]], base=0, channel_multiplier=0,
                   allow_small_or_imprecise_dtypes=True).then_inc(made, 1)
            pool.wait_ge(made, 1)
            g.affine_select(out=ident[:, :], in_=ident[:, :], compare_op=ALU.not_equal, fill=1.0, base=0,
                            pattern=[[-1, P]], channel_multiplier=1).then_inc(made, 1)

            def low_half(m, n):
                pool.wait_ge(high_done, n + 1)
                g.tensor_tensor(w_low[:, m % PAIRS, :], raw[:, m, :], w_high[:, m % PAIRS, :].bitcast(F32),
                                ALU.subtract).then_inc(low_done, 1)

            def low_halves(L):
                for m in range(RAW):
                    low_half(m, L * PARTS + m)
                    if L and m == QUARTERS:
                        pool.wait_ge(sgu_in, 32)
                        g.affine_select(out=sguraw, in_=sguraw, compare_op=ALU.is_ge, fill=0.0, base=0,
                                        pattern=[[0, HEADS], [-1, P]], channel_multiplier=1).then_inc(sgu_masked, 1)
                with pool.Fori(1, PARTS // RAW - 1) as i:
                    for m in range(RAW):
                        low_half(m, i * RAW + (L * PARTS + m))

            def gather_u(L, b, i, j):
                listed = [(experts_u, i + ((L * BLOCKS + b) * HEADS + 2))] if j == 0 else []
                before = L * SLOTS_FREED_U + b * HEADS * TOPK
                wait_unfused(pool, *listed, (u_free, i * TOPK + (before + j + 1)))
                g.indirect_dma_start(
                    out=uslot[j % USLOTS], out_offset=None, in_=peer_u.rearrange("l e d -> (l e) d"),
                    in_offset=bass.IndirectOffsetOnAxis(ap=expert_u[:, j:j + 1], axis=0),
                ).then_inc(u_in[j % USLOTS], 16)

            def gather_v(L, b, i, j):
                listed = [(experts_v, i + ((L * BLOCKS + b) * HEADS + 1))] if j == 0 else []
                before = L * SLOTS_FREED_V + b * HEADS * TOPK
                wait_unfused(pool, *listed, (v_free, i * TOPK + (before + j + 1)))
                g.indirect_dma_start(
                    out=vslot[j % VSLOTS], out_offset=None, in_=peer_v.rearrange("l e d -> (l e) d"),
                    in_offset=bass.IndirectOffsetOnAxis(ap=expert_v[:, j:j + 1], axis=0),
                ).then_inc(v_in[j % VSLOTS], 16)

            def experts(L):
                for j in range(TOPK):
                    if j < RAW:
                        low_half(j, (L + 1) * PARTS - RAW + j)
                    gather_u(L, 0, 0, j)
                for j in range(TOPK):
                    gather_v(L, 0, 0, j)
                for b in range(BLOCKS):
                    with pool.Fori(1 - b, HEADS) as i:
                        for j in range(TOPK):
                            gather_u(L, b, i, j)
                        for j in range(TOPK):
                            gather_v(L, b, i, j)

            low_halves(0)
            experts(0)
            low_halves(1)
            experts(1)

        @block.tensor
        def _(pe):
            mm = nc.tensor.matmul

            def transposes(m):
                for b in range(BLOCKS):
                    pe.wait_ge(scale_ready, BLOCKS * m + b + 1)
                    for k in range(KD):
                        at = (k % 2) * SEQ + b * P
                        last = mm(ps[:, k // 2, at:at + P], h[:, b, k * P:(k + 1) * P], scale[b], start=True, stop=True)
                        if b == BLOCKS - 1 and k % 2:
                            last.then_inc(turned, 1)

            def three_passes(o, left, right, start, stop):
                mm(o, left[0], right[0], start=start, stop=False)
                mm(o, left[0], right[1], start=False, stop=False)
                return mm(o, left[1], right[0], start=False, stop=stop)

            def channel_bank(t, parts_before, i=0, norm=None):
                for q in range(QUARTERS):
                    high, low = (w[:, q, :].rearrange("p (k c) -> p k c", c=WCOLS) for w in (w_high, w_low))
                    pe.wait_ge(low_done, i + (parts_before + q + 1))
                    if norm is not None:
                        pe.wait_ge(zT_split, norm * KD // 2 + 2 * (q + 1))
                    for c in range(WCOLS // P):
                        cs = slice(c * P, (c + 1) * P)
                        for k in range(4):
                            kz = 4 * q + k
                            last = three_passes(ps[:, t, c * SEQ:(c + 1) * SEQ],
                                                (high[:, k, cs], low[:, k, cs]),
                                                (zT_high[:, kz, :], zT_low[:, kz, :]),
                                                start=(q == 0 and c == 0 and k == 0),
                                                stop=(q == QUARTERS - 1 and c == 1 and k == 3))
                    last.then_inc(pair_free, 1)

            pe.wait_ge(made, CONSTANTS)
            pe.wait_ge(rows_in, 16 * 9)
            nc.tensor.transpose(ps[:, 6, 0:ROWS_A], paramrow[0:ROWS_A, 0, :], ident[0:ROWS_A, 0:ROWS_A])
            for a in range(2):
                last = nc.tensor.transpose(ps[:, 6, (a + 1) * P:(a + 1) * P + ROWS_B], paramrow[0:ROWS_B, a + 1, :],
                                           ident[0:ROWS_B, 0:ROWS_B])
            last.then_inc(params_turned, 1)

            for L in range(LAYERS):
                if L:
                    pe.wait_ge(h_expert, BLOCKS * L)
                else:
                    pe.wait_ge(cols_ready, 3)
                transposes(2 * L)
                pe.wait_ge(tile_out, BANKS * L + 1)
                channel_bank(0, RAW + L * PARTS, norm=2 * L)
                pe.wait_ge(keys_in, 16 * (L + 1))
                for hd in range(HEADS):
                    last = nc.tensor.transpose(ps[:, 4 + hd // 4, (hd % 4) * P:(hd % 4 + 1) * P], subraw[:, hd, :],
                                               ident[:, :])
                last.then_inc(keys_turned, 1)
                if L == 0:
                    for t in range(1, 4):
                        pe.wait_ge(tile_out, t + 1)
                        channel_bank(t, RAW + t * QUARTERS)
                    with pe.Fori(1, 4) as i:
                        for t in range(4):
                            pe.wait_ge(tile_out, i * 4 + (t + 1))
                            channel_bank(t, RAW + t * QUARTERS, i * 4 * QUARTERS)
                    pe.wait_ge(shared_in, 16)
                    pe.wait_ge(keys_ready, 2)
                    for gr in range(len(WINDOWS)):
                        pe.wait_ge(pooled, gr + 1)
                        for dd in range(2):
                            for kc in range(2):
                                last = mm(ps[:, 4 + gr, dd * SEQ:(dd + 1) * SEQ],
                                          poolw[:, 2 * gr + kc, dd * P:(dd + 1) * P], proj[:, 2 * gr + kc, :],
                                          start=(kc == 0), stop=(kc == 1))
                        last.then_inc(pool_mixed, 1)
                else:
                    pe.wait_ge(sgu_masked, 1)
                    for hd in range(HEADS):
                        last = nc.tensor.transpose(ps[:, 6 + hd // 4, (hd % 4) * P:(hd % 4 + 1) * P],
                                                   sguraw[:, hd, :], ident[:, :])
                    last.then_inc(sgu_turned, 1)
                    bank0 = BANKS * L
                    for t in range(1, 8):
                        pe.wait_ge(tile_out, bank0 + t + 1)
                        channel_bank(t % 4, RAW + L * PARTS + t * QUARTERS)
                    for t in range(4):
                        pe.wait_ge(tile_out, bank0 + 8 + t + 1)
                        for q in range(QUARTERS):
                            high, low = (w[:, q, :].rearrange("p (k c) -> p k c", c=WCOLS) for w in (w_high, w_low))
                            pe.wait_ge(low_done, RAW + L * PARTS + (8 + t) * QUARTERS + q + 1)
                            for b in range(BLOCKS):
                                for k in range(4):
                                    kz = 4 * q + k
                                    last = three_passes(ps[:, t, b * WCOLS:(b + 1) * WCOLS],
                                                        (zT_high[:, kz, b * P:(b + 1) * P],
                                                         zT_low[:, kz, b * P:(b + 1) * P]),
                                                        (high[:, k, :], low[:, k, :]),
                                                        start=(q == 0 and b == 0 and k == 0),
                                                        stop=(q == QUARTERS - 1 and b == 1 and k == 3))
                            last.then_inc(pair_free, 1)
                    for t in range(4):
                        pe.wait_ge(tile_out, bank0 + 12 + t + 1)
                        channel_bank(t, RAW + L * PARTS + (12 + t) * QUARTERS)
                        if t == 0:
                            pe.wait_ge(keys_ready, 4)
                            pe.wait_ge(sgu_copied, 2)
                            for c2 in range(CH // 2):
                                pe.wait_ge(conv_summed, c2 + 1)
                                mm(ps[:, 4 + c2, :], mean_of[:, :], proj[:, 2 * c2:2 * c2 + 2, :],
                                   start=True, stop=True).then_inc(gn_mean, 1)
                        if t == 1:
                            for c2 in range(CH // 2):
                                pe.wait_ge(gn_squared, c2 + 1)
                                mm(ps[:, 4 + c2, :], mean_of[:, :], proj[:, 2 * c2:2 * c2 + 2, :],
                                   start=True, stop=True).then_inc(gn_var, 1)
                        if t == 2:
                            pe.wait_ge(v_ready, BLOCKS)
                            for hd in range(HEADS):
                                if hd % 2 == 0:
                                    pe.wait_ge(gn_root, hd // 2 + 1)
                                for b in range(BLOCKS):
                                    o = ps[:, 4 + hd // 2, (hd % 2) * SEQ + b * P:(hd % 2) * SEQ + (b + 1) * P]
                                    mm(o, ones_row[0:1, :], sgub[0:1, hd * P:(hd + 1) * P], start=True, stop=False)
                                    last = mm(o, vt[:, b, hd * P:(hd + 1) * P], wmT[:, hd, :],
                                              start=False, stop=True)
                                if hd % 2:
                                    last.then_inc(gated, 1)
                chunks = [first + c for first, _ in ROW_ORDER[L] for c in range(CH)]
                for n2, k in enumerate(chunks):
                    if n2 == 0:
                        if L == 0:
                            pe.wait_ge(y_split, len(WINDOWS))
                        else:
                            pe.wait_ge(sgu_out, CH // 2)
                        pe.wait_ge(tile_out, 4 + BANKS * L + IN_GROUPS)
                    pe.wait_ge(y_split, CH * L + n2 // 2 + 1)
                    for half in range(2):
                        n = 2 * n2 + half
                        pe.wait_ge(low_done, RAW + L * PARTS + IN_GROUPS * QUARTERS + n + 1)
                        for b in range(BLOCKS):
                            bs = slice(b * P, (b + 1) * P)
                            for q in range(2):
                                cs = slice(q * BANK, (q + 1) * BANK)
                                last = three_passes(ps[:, 4 * b + 2 * half + q, :],
                                                    (zT_high[:, k, bs], zT_low[:, k, bs]),
                                                    (w_high[:, n % PAIRS, cs], w_low[:, n % PAIRS, cs]),
                                                    start=(n2 == 0), stop=(n2 == KD - 1))
                        last.then_inc(pair_free, 1)

                pe.wait_ge(h_mixed, 8 * (L + 1))
                transposes(2 * L + 1)
                def score(b, t, heads=2):
                    pe.wait_ge(tile_out, 4 + BANKS * L + IN_GROUPS + t + 1)
                    for hd in range(2 * t + 2 - heads, 2 * t + 2):
                        o = ps[:, 4 * (1 - b) + t, (hd % 2) * SEL:(hd % 2 + 1) * SEL]
                        last = mm(o, qT[:, hd, b * P:(b + 1) * P], subT[:, hd, :], start=True, stop=True)
                    last.then_inc(q_scored, 1)

                pe.wait_ge(tile_out, BANKS * L + IN_GROUPS + 1)
                for c, bank in ((0, 0), (1, 7)):
                    cs = slice(c * P, (c + 1) * P)
                    for q in range(QUARTERS):
                        high, low = (w[:, q, :].rearrange("p (k c) -> p k c", c=WCOLS) for w in (w_high, w_low))
                        if c == 0:
                            pe.wait_ge(low_done, RAW + L * PARTS + Q_AT + q + 1)
                            pe.wait_ge(zT_split, (2 * L + 1) * KD // 2 + 2 * (q + 1))
                        for k in range(4):
                            kz = 4 * q + k
                            last = three_passes(ps[:, bank, 0:SEQ], (high[:, k, cs], low[:, k, cs]),
                                                (zT_high[:, kz, :], zT_low[:, kz, :]),
                                                start=(q == 0 and k == 0), stop=(q == QUARTERS - 1 and k == 3))
                        if c == 1:
                            last.then_inc(pair_free, 1)
                        if (c, q) == (0, QUARTERS - 1):
                            last.then_inc(first_query, 1)
                        if (c, q) == (1, 1):
                            pe.wait_ge(first_copied, L + 1)
                            mm(ps[:, 4, 0:SEL], qT[:, 0, 0:P], subT[:, 0, :], start=True, stop=True)\
                                .then_inc(first_scored, 1)
                pe.wait_ge(head_in, L * BLOCKS * HEADS + 1)
                score(0, 0, heads=1)
                for t in range(1, 4):
                    pe.wait_ge(tile_out, BANKS * L + IN_GROUPS + t + 1)
                    channel_bank(t, RAW + L * PARTS + Q_AT + t * QUARTERS)
                for t in range(1, 4):
                    score(0, t)
                for t in range(4):
                    score(1, t)
                for b in range(BLOCKS):
                    pe.wait_ge(scores_out, (L + 1) * BLOCKS * HEADS // 2)
                    for q in range(D // BANK):
                        mm(ps[:, 4 * b + q, :], ident[:, :], h[:, b, q * BANK:(q + 1) * BANK],
                           start=True, stop=False)
                    rows = (L * BLOCKS + b) * HEADS * TOPK

                    def add_rows(i, js):
                        for j in js:
                            pe.wait_ge(diag_done, i * TOPK + (rows + j + 1))
                            per = TOPK // VSLOTS
                            pe.wait_ge(v_in[j % VSLOTS],
                                       i * (16 * per) + 16 * (rows // VSLOTS + j // VSLOTS + 1))
                            for q in range(D // BANK):
                                last = mm(ps[:, 4 * b + q, :], diag[:, j, :],
                                          vslot[j % VSLOTS][:, q * BANK:(q + 1) * BANK], start=False, stop=False)
                            last.then_inc(v_free, 1)

                    with pe.Fori(0, HEADS - b) as i:
                        add_rows(i, range(TOPK))
                    if b:
                        add_rows(HEADS - 1, [j for j in range(TOPK) if j not in DVE_ROWS])
                    for q in range(D // BANK):
                        last = mm(ps[:, 4 * b + q, :], zeros[:, :],
                                  zeros[:, 0:1].to_broadcast([P, BANK]), start=False, stop=True)
                    last.then_inc(block_done, 1)

        @block.scalar
        def _(act):
            a = nc.scalar.activation

            def norm_root(m, b):
                a(xn[:, b, :], h[:, b, :], ACT.Square, accum_out=square_sum[:, b:b + 1]).then_inc(squared, 1)
                act.wait_ge(squared, BLOCKS * m + b + 1)
                a(root[:, b:b + 1], square_sum[:, b:b + 1], ACT.Sqrt, scale=1.0 / D, bias=eps_col[:, :])\
                    .then_inc(rooted, 1)

            def sqrt_table():
                a(table[:, :], eps_col[:, :], ACT.Sqrt).then_inc(table_used, 1)
                uses[0] += 1
                act.wait_ge(table_used, uses[0])

            uses = [0]

            def norm_rows(m, gain_at, between=None):
                for kk in range(KD // 2):
                    if between is not None and kk % 2 == 0:
                        between(kk // 2)
                    act.wait_ge(turned, (KD // 2) * m + kk + 1)
                    for k in (2 * kk, 2 * kk + 1):
                        last = a(zT_high[:, k, :], ps[:, kk, (k % 2) * SEQ:(k % 2 + 1) * SEQ], ACT.Copy,
                                 scale=colA[:, gain_at + k:gain_at + k + 1])
                    last.then_inc(zT_rounded, 1)

            def high_part(L, group, odd, q, i=0):
                slot = QUARTERS * odd + q
                n = L * PARTS + group * QUARTERS + q
                act.wait_ge(raw_in[slot], i * 16 + 16 * (n // RAW + 1))
                act.wait_ge(pair_free, i * RAW + (n + 1))
                a(w_high[:, q, :], raw[:, slot, :], ACT.Copy).then_inc(high_done, 1)

            def high_group(L, group, odd, i=0, between=None):
                for q in range(QUARTERS):
                    if between is not None and q == QUARTERS - 1:
                        between()
                    high_part(L, group, odd, q, i)

            def bank_out(t, out_, func, used):
                act.wait_ge(pair_free, used)
                a(out_, ps[:, t, :].rearrange("p (c t) -> p c t", c=2), func).then_inc(tile_out, 1)

            def v_squares():
                act.wait_ge(v_centred, BLOCKS)
                for b in range(BLOCKS):
                    a(padded[:, 4 * b:4 * b + 4, 0:SEQ], vt[:, b, :].rearrange("p (c t) -> p c t", c=4), ACT.Square,
                      accum_out=vstat[:, 1, b:b + 1]).then_inc(v_squared, 1)
                act.wait_ge(v_squared, BLOCKS)
                a(vstat[:, 2, :], vstat[:, 1, :], ACT.Sqrt, scale=1.0 / SECTION, bias=eps_col[:, :])\
                    .then_inc(v_root, 1)

            def group_squares():
                for c2 in range(CH // 2):
                    act.wait_ge(gn_centred, c2 + 1)
                    a(proj[:, 2 * c2:2 * c2 + 2, :], proj[:, CH + 2 * c2:CH + 2 * c2 + 2, :], ACT.Square)\
                        .then_inc(gn_squared, 1)

            def group_roots():
                for c2 in range(CH // 2):
                    act.wait_ge(gn_var, c2 + 1)
                    a(proj[:, 2 * c2:2 * c2 + 2, :], ps[:, 4 + c2, :].rearrange("p (c t) -> p c t", c=2),
                      ACT.Sqrt, bias=eps_col[:, :]).then_inc(gn_root, 1)

            def group_output(chunks):
                for c in chunks:
                    act.wait_ge(gn_scaled, c // 2 + 1)
                    a(proj[:, CH + c, :], proj[:, CH + c, :], ACT.Silu,
                      scale=colA[:, ROWS_GNG + c:ROWS_GNG + c + 1],
                      bias=colA[:, ROWS_GNB + c:ROWS_GNB + c + 1]).then_inc(gn_out, 1)

            def group_rounded():
                for c2 in range(CH // 2):
                    act.wait_ge(gn_out, 2 * c2 + 2)
                    a(zT_high[:, CH + 2 * c2:CH + 2 * c2 + 2, :], proj[:, CH + 2 * c2:CH + 2 * c2 + 2, :],
                      ACT.Copy).then_inc(y_rounded, 1)

            act.wait_ge(made, CONSTANTS)
            sqrt_table()
            act.wait_ge(x_in, 16 * BLOCKS)
            for b in range(BLOCKS):
                norm_root(0, b)
            act.wait_ge(params_turned, 1)
            a(colA[:, :], ps[:, 6, 0:ROWS_A], ACT.Copy).then_inc(cols_ready, 1)
            for s in range(2):
                a(convT[:, s * ROWS_B:(s + 1) * ROWS_B], ps[:, 6, (s + 1) * P:(s + 1) * P + ROWS_B], ACT.Copy)\
                    .then_inc(cols_ready, 1)
            act.wait_ge(cols_ready, 3)
            for L in range(LAYERS):
                norm_rows(2 * L, ROWS_MIX + KD * L, lambda q: high_part(L, 0, 0, q))
                used = PAIRS + L * PARTS

                def keys_out():
                    act.wait_ge(keys_turned, L + 1)
                    for p2 in range(2):
                        rows = slice(64 * p2, 64 * p2 + 64)
                        a(subT[rows, :, p2 * NKEYS:(p2 + 1) * NKEYS],
                          ps[rows, 4:6, :].rearrange("p a (h n) -> p (a h) n", n=NKEYS), ACT.Copy)\
                            .then_inc(keys_ready, 1)

                if L == 0:
                    for t in range(4):
                        high_group(L, t + 1, (t + 1) % 2)
                        bank_out(t, proj[:, 2 * t:2 * t + 2, :], ACT.Copy, used + (t + 1) * QUARTERS)
                        if t == 0:
                            keys_out()
                    with act.Fori(1, 4) as i:
                        for t in range(4):
                            odd = (t + 1) % 2
                            high_group(L, t + 1, odd, i * 2)
                            value = i * (4 * QUARTERS) + (used + (t + 1) * QUARTERS)
                            wait_unfused(act, (pair_free, value))
                            a(proj[:, bass.ds(i * CH + 2 * t, 2), :],
                              ps[:, t, :].rearrange("p (c t) -> p c t", c=2), ACT.Copy).then_inc(tile_out, 1)
                    for gr in range(len(WINDOWS)):
                        act.wait_ge(pool_mixed, gr + 1)
                        for dd in range(2):
                            c = 2 * gr + dd
                            last = a(zT_high[:, c, :], ps[:, 4 + gr, dd * SEQ:(dd + 1) * SEQ], ACT.Copy,
                                     scale=colA[:, ROWS_SCALE + c:ROWS_SCALE + c + 1])
                        last.then_inc(y_rounded, 1)
                    for c2 in range(CH // 2):
                        act.wait_ge(conv_out, c2 + 1)
                        a(zT_high[:, CH + 2 * c2:CH + 2 * c2 + 2, :], proj[:, CH + 2 * c2:CH + 2 * c2 + 2, :],
                          ACT.Copy).then_inc(y_rounded, 1)
                else:
                    for group in range(IN_GROUPS):
                        high_group(L, group + 1, (group + 1) % 2,
                                   between={13: group_squares, 15: lambda: group_output(range(CH // 2, CH))}.get(group))
                        done = used + (group + 1) * QUARTERS
                        t = group % 4
                        if group < 8:
                            at = (group % 2) * CH + 2 * (group // 2)
                            bank_out(t, proj[:, at:at + 2, :], (ACT.Copy, ACT.Sigmoid)[group % 2], done)
                        elif group < 12:
                            act.wait_ge(pair_free, done)
                            for b in range(BLOCKS):
                                last = a(vt[:, b, t * WCOLS:(t + 1) * WCOLS], ps[:, t, b * WCOLS:(b + 1) * WCOLS],
                                         ACT.Gelu, accum_out=vsum[:, b, t:t + 1])
                            last.then_inc(tile_out, 1)
                        else:
                            act.wait_ge(conv_summed, CH // 2)
                            bank_out(t, proj[:, 2 * CH + 2 * t:2 * CH + 2 * t + 2, :], ACT.Gelu, done)
                        if group == 0:
                            keys_out()
                            act.wait_ge(sgu_turned, 1)
                            for s in range(2):
                                a(wmT[:, 4 * s:4 * s + 4, :], ps[:, 6 + s, :].rearrange("p (h t) -> p h t", h=4),
                                  ACT.Copy).then_inc(sgu_copied, 1)
                        if group == 12:
                            v_squares()
                        if group == 13:
                            group_roots()
                        if group == 14:
                            group_output(range(CH // 2))
                    group_rounded()
                    for c2 in range(CH // 2):
                        act.wait_ge(sgu_out, c2 + 1)
                        a(zT_high[:, 2 * c2:2 * c2 + 2, :], proj[:, 2 * CH + 2 * c2:2 * CH + 2 * c2 + 2, :], ACT.Copy)\
                            .then_inc(y_rounded, 1)

                for group in range(IN_GROUPS + 1, IN_GROUPS + OUT_GROUPS + 1):
                    high_group(L, group, group % 2)
                sqrt_table()
                for b in range(BLOCKS):
                    act.wait_ge(h_mixed, 8 * L + 4 * (b + 1))
                    norm_root(2 * L + 1, b)
                norm_rows(2 * L + 1, ROWS_FFN + KD * L)
                def copy_scores(source):
                    a(sc, source, ACT.Copy).then_inc(head_in, 1)

                def exponentials(i, heads):
                    act.wait_ge(under_max, i + (heads + 1))
                    a(expo[:, :], below[:, :], ACT.Exp, accum_out=denom[:, 0:1]).then_inc(exp_done, 1)

                def weighting(i, b, heads):
                    act.wait_ge(u_free, i * TOPK + (L * SLOTS_FREED_U + USLOTS + (b * HEADS + 1) * TOPK))
                    a(gelu[:, :], dots[:, :], ACT.Gelu).then_inc(gelu_done, 1)
                    act.wait_ge(weights_done, i + (heads + 1))
                    act.wait_ge(v_free, i * TOPK + (L * SLOTS_FREED_V + VSLOTS + b * HEADS * TOPK))
                    for j in range(TOPK):
                        a(diag[:, j, :], ident[:, :], ACT.Copy, scale=weight[:, j:j + 1]).then_inc(diag_done, 1)

                for t in range(4):
                    group = IN_GROUPS + OUT_GROUPS + t
                    if t == 0:
                        act.wait_ge(first_query, L + 1)
                        a(qT[:, 0, :], ps[:, 0, 0:SEQ], ACT.Copy).then_inc(first_copied, 1)
                        high_part(L, group + 1, (group + 1) % 2, 0)
                        act.wait_ge(first_scored, L + 1)
                        act.wait_ge(experts_u, L * BLOCKS * HEADS + 1)
                        copy_scores(ps[:, 4, 0:SEL].rearrange("p (x n) -> p x n", x=2))
                        for q in range(1, QUARTERS):
                            high_part(L, group + 1, (group + 1) % 2, q)
                        act.wait_ge(pair_free, used + (group + 1) * QUARTERS)
                        a(qT[:, 1, :], ps[:, 7, 0:SEQ], ACT.Copy).then_inc(tile_out, 1)
                        continue
                    if t < 3:
                        high_group(L, group + 1, (group + 1) % 2)
                    bank_out(t, qT[:, 2 * t:2 * t + 2, :], ACT.Copy, used + (group + 1) * QUARTERS)
                    if t == 2:
                        exponentials(0, L * BLOCKS * HEADS)
                for b in range(BLOCKS):
                    for t in range(4):
                        act.wait_ge(q_scored, L * HEADS + b * 4 + t + 1)
                        a(scores[:, b, 2 * t:2 * t + 2, :],
                          ps[:, 4 * (1 - b) + t, :].rearrange("p (h n) -> p h n", h=2), ACT.Copy).then_inc(scores_out, 1)
                act.wait_ge(scores_out, (L + 1) * HEADS)
                a(freed_by_act[:, L:L + 1], eps_col[:, :], ACT.Copy).then_inc(v_free, VSLOTS)

                def block_out(b):
                    sqrt_table()
                    if b == 0:
                        act.wait_ge(block_done, L * BLOCKS + b + 1)
                        a(h[:, b, :], ps[:, 4 * b:4 * b + 4, :].rearrange("p a n -> p (a n)"), ACT.Copy)\
                            .then_inc(h_expert, 1)
                    act.wait_ge(h_expert, L * BLOCKS + b + 1)
                    norm_root(2 * (L + 1), b)

                for b in range(BLOCKS):
                    heads = (L * BLOCKS + b) * HEADS
                    if b:
                        act.wait_ge(experts_u, heads + 1)
                        copy_scores(scores[:, b, 0:1, :].rearrange("p a (x n) -> p (a x) n", x=2))
                        exponentials(0, heads)
                        block_out(b - 1)
                    weighting(0, b, heads)
                    with act.Fori(1, HEADS) as i:
                        wait_unfused(act, (experts_u, i + (heads + 1)))
                        copy_scores(scores[:, b, bass.ds(i, 1), :].rearrange("p a (x n) -> p (a x) n", x=2))
                        exponentials(i, heads)
                        weighting(i, b, heads)
                block_out(BLOCKS - 1)

        @block.vector
        def _(dve):
            v = nc.vector
            steps = [0]

            def step(ins):
                steps[0] += 1
                ins.then_inc(dve_step, 1)
                dve.wait_ge(dve_step, steps[0])

            def norm_scale(m, b):
                dve.wait_ge(rooted, BLOCKS * m + b + 1)
                v.reciprocal(rstd[:, b:b + 1], root[:, b:b + 1]).then_inc(rstd_ready, 1)
                dve.wait_ge(rstd_ready, BLOCKS * m + b + 1)

            def norm_rows(m, gain_at):
                for b in range(BLOCKS):
                    norm_scale(m, b)
                    v.tensor_scalar(scale[b], ident[:, :], rstd[:, b:b + 1], None, ALU.mult)\
                        .then_inc(scale_ready, 1)
                for kk in range(KD // 2):
                    dve.wait_ge(zT_rounded, (KD // 2) * m + kk + 1)
                    for k in (2 * kk, 2 * kk + 1):
                        last = v.scalar_tensor_tensor(zT_low[:, k, :], ps[:, kk, (k % 2) * SEQ:(k % 2 + 1) * SEQ],
                                                      colA[:, gain_at + k:gain_at + k + 1],
                                                      zT_high[:, k, :].bitcast(F32), ALU.mult, ALU.subtract)
                    last.then_inc(zT_split, 1)

            def split_y(n, at, exact):
                dve.wait_ge(y_rounded, n + 1)
                v.tensor_tensor(zT_low[:, at:at + 2, :], exact, zT_high[:, at:at + 2, :].bitcast(F32),
                                ALU.subtract).then_inc(y_split, 1)

            v.memset(token[:, 0:1], 0.0).then_inc(low_done, RAW)
            v.memset(token[:, 1:2], 0.0).then_inc(tile_out, 4)
            v.memset(token[:, 2:3], 0.0).then_inc(pair_free, PAIRS)
            v.memset(token[:, 3:4], 0.0).then_inc(experts_u, 1)
            dve.wait_ge(made, CONSTANTS)

            for L in range(LAYERS):
                norm_rows(2 * L, ROWS_MIX + KD * L)
                if L == 0:
                    dve.wait_ge(keys_turned, 1)
                    step(v.memset(padpool[:, :, :, 0:WINDOWS[-1]], 0.0))
                    for gr, window in enumerate(WINDOWS):
                        step(v.tensor_scalar(inv_count[:, :], position[:, :], float(window), None, ALU.min))
                        step(v.reciprocal(inv_count[:, :], inv_count[:, :]))
                        dve.wait_ge(tile_out, 4 + gr + 1)
                        own = proj[:, 2 * gr:2 * gr + 2, :]
                        W0 = WINDOWS[-1]
                        step(v.tensor_copy(padpool[:, 0, :, W0:], own))
                        lag, at = 1, 0
                        while lag < window:
                            step(v.tensor_tensor(padpool[:, 1 - at, :, W0:], padpool[:, at, :, W0:],
                                                 padpool[:, at, :, W0 - lag:W0 - lag + SEQ], ALU.add))
                            lag, at = 2 * lag, 1 - at
                        step(v.tensor_tensor(padpool[:, at, :, W0:], padpool[:, at, :, W0:],
                                             inv_count[:, None, :].to_broadcast([P, 2, SEQ]), ALU.mult))
                        v.tensor_tensor(own, padpool[:, at, :, W0:], own, ALU.subtract).then_inc(pooled, 1)
                    dve.wait_ge(pooled, len(WINDOWS))
                    edge = SHORT - 1
                    step(v.memset(padshort[:, :, 0:edge], 0.0))
                    for t in range(4):
                        dve.wait_ge(tile_out, 4 + 12 + t + 1)
                        cs = slice(2 * t, 2 * t + 2)
                        step(v.tensor_tensor(padshort[:, cs, edge:], proj[:, 2 * CH + 2 * t:2 * CH + 2 * t + 2, :],
                                             proj[:, 3 * CH + 2 * t:3 * CH + 2 * t + 2, :], ALU.mult))
                        tap = lambda k, c: colA[:, ROWS_SHORT + k * CH + c:ROWS_SHORT + k * CH + c + 1]
                        acc = lambda c: proj[:, 2 * CH + c, :]
                        for c in (2 * t, 2 * t + 1):
                            step(v.tensor_scalar(acc(c), padshort[:, c, 0:SEQ], tap(0, c), None, ALU.mult))
                        for k in range(1, SHORT):
                            for c in (2 * t, 2 * t + 1):
                                step(v.scalar_tensor_tensor(acc(c), padshort[:, c, k:k + SEQ], tap(k, c), acc(c),
                                                            ALU.mult, ALU.add))
                        v.tensor_tensor(proj[:, CH + 2 * t:CH + 2 * t + 2, :], proj[:, CH + 2 * t:CH + 2 * t + 2, :],
                                        proj[:, 2 * CH + 2 * t:2 * CH + 2 * t + 2, :], ALU.mult).then_inc(conv_out, 1)
                    for gr in range(len(WINDOWS)):
                        dve.wait_ge(y_rounded, gr + 1)
                        for dd in range(2):
                            c = 2 * gr + dd
                            last = v.scalar_tensor_tensor(zT_low[:, c, :], ps[:, 4 + gr, dd * SEQ:(dd + 1) * SEQ],
                                                          colA[:, ROWS_SCALE + c:ROWS_SCALE + c + 1],
                                                          zT_high[:, c, :].bitcast(F32), ALU.mult, ALU.subtract)
                        last.then_inc(y_split, 1)
                    for c2 in range(CH // 2):
                        split_y(4 + c2, CH + 2 * c2, proj[:, CH + 2 * c2:CH + 2 * c2 + 2, :])
                else:
                    TB = 4 + BANKS * L
                    edge = TAPS - 1
                    dve.wait_ge(keys_turned, 2)
                    dve.wait_ge(sgu_turned, 1)
                    step(v.memset(padded[:, :, 0:edge], 0.0))
                    for t in range(4):
                        dve.wait_ge(tile_out, TB + 2 * t + 2)
                        cs = slice(2 * t, 2 * t + 2)
                        step(v.tensor_tensor(padded[:, cs, edge:], proj[:, cs, :],
                                             proj[:, CH + 2 * t:CH + 2 * t + 2, :], ALU.mult))
                        before = t * TAPS * 2
                        sums = [(proj[:, odd * 2 * CH + c, :], odd, c) for odd in range(2) for c in (2 * t, 2 * t + 1)]
                        for sum_, odd, c in sums:
                            if odd:
                                first = v.tensor_scalar(sum_, padded[:, c, 1:1 + SEQ], convT[:, CH + c:CH + c + 1],
                                                        None, ALU.mult)
                            else:
                                first = v.tensor_scalar(sum_, padded[:, c, 0:SEQ], convT[:, c:c + 1],
                                                        colA[:, ROWS_CONVB + c:ROWS_CONVB + c + 1], ALU.mult, ALU.add)
                            first.then_inc(conv_step, 1)
                        with dve.Fori(1, TAPS // 2) as k:
                            for n, (sum_, odd, c) in enumerate(sums):
                                dve.wait_ge(conv_step, k * 4 + (before + n - 3))
                                v.scalar_tensor_tensor(sum_, padded[:, c, bass.ds(k * 2 + odd, SEQ)],
                                                       convT[:, bass.ds(k * 2 * CH + (odd * CH + c), 1)], sum_,
                                                       ALU.mult, ALU.add).then_inc(conv_step, 1)
                        for n, (sum_, odd, c) in enumerate(sums[0:2]):
                            dve.wait_ge(conv_step, before + 4 * (TAPS // 2) - 3 + n)
                            v.scalar_tensor_tensor(sum_, padded[:, c, TAPS - 1:TAPS - 1 + SEQ],
                                                   convT[:, (TAPS - 1) * CH + c:(TAPS - 1) * CH + c + 1], sum_,
                                                   ALU.mult, ALU.add).then_inc(conv_step, 1)
                        dve.wait_ge(conv_step, before + TAPS * 2)
                        v.tensor_tensor(proj[:, cs, :], proj[:, cs, :], proj[:, 2 * CH + 2 * t:2 * CH + 2 * t + 2, :],
                                        ALU.add).then_inc(conv_summed, 1)
                    dve.wait_ge(tile_out, TB + 12)
                    dve.wait_ge(shared_in, 48)
                    step(v.tensor_reduce(vstat[:, 0, :], vsum[:, :, :], AX.X, ALU.add))
                    step(v.tensor_scalar(vstat[:, 0, :], vstat[:, 0, :], 1.0 / SECTION, None, ALU.mult))
                    for b in range(BLOCKS):
                        v.tensor_scalar(vt[:, b, :], vt[:, b, :], vstat[:, 0, b:b + 1], None, ALU.subtract)\
                            .then_inc(v_centred, 1)
                    dve.wait_ge(v_root, 1)
                    step(v.reciprocal(vstat[:, 3, :], vstat[:, 2, :]))
                    for b in range(BLOCKS):
                        step(v.scalar_tensor_tensor(vt[:, b, :], vt[:, b, :], vstat[:, 3, b:b + 1], vgb[:, 0, :],
                                                    ALU.mult, ALU.mult))
                        v.tensor_tensor(vt[:, b, :], vt[:, b, :], vgb[:, 1, :], ALU.add).then_inc(v_ready, 1)
                    for c2 in range(CH // 2):
                        cs = slice(2 * c2, 2 * c2 + 2)
                        dve.wait_ge(gn_mean, c2 + 1)
                        v.tensor_tensor(proj[:, CH + 2 * c2:CH + 2 * c2 + 2, :], proj[:, cs, :],
                                        ps[:, 4 + c2, :].rearrange("p (c t) -> p c t", c=2), ALU.subtract)\
                            .then_inc(gn_centred, 1)
                    for c2 in range(CH // 2):
                        cs = slice(2 * c2, 2 * c2 + 2)
                        zs = slice(CH + 2 * c2, CH + 2 * c2 + 2)
                        dve.wait_ge(gn_root, c2 + 1)
                        step(v.reciprocal(proj[:, cs, :], proj[:, cs, :]))
                        v.tensor_tensor(proj[:, zs, :], proj[:, zs, :], proj[:, cs, :], ALU.mult)\
                            .then_inc(gn_scaled, 1)
                    for c2 in range(CH // 2):
                        dve.wait_ge(gated, c2 + 1)
                        dve.wait_ge(tile_out, TB + 12 + c2 + 1)
                        v.tensor_tensor(proj[:, 2 * CH + 2 * c2:2 * CH + 2 * c2 + 2, :],
                                        proj[:, 2 * CH + 2 * c2:2 * CH + 2 * c2 + 2, :],
                                        ps[:, 4 + c2, :].rearrange("p (c t) -> p c t", c=2), ALU.mult)\
                            .then_inc(sgu_out, 1)
                    for c2 in range(CH // 2):
                        split_y(CH + c2, CH + 2 * c2, proj[:, CH + 2 * c2:CH + 2 * c2 + 2, :])
                    for c2 in range(CH // 2):
                        split_y(CH + 4 + c2, 2 * c2, proj[:, 2 * CH + 2 * c2:2 * CH + 2 * c2 + 2, :])

                dve.wait_ge(pair_free, PAIRS + L * PARTS + Q_AT)
                for b in range(BLOCKS):
                    for q in range(D // BANK):
                        s = slice(q * BANK, (q + 1) * BANK)
                        v.tensor_tensor(h[:, b, s], ps[:, 4 * b + q, :], h[:, b, s], ALU.add).then_inc(h_mixed, 1)
                norm_rows(2 * L + 1, ROWS_FFN + KD * L)
                dve.wait_ge(gain_in, 16 * (L + 1))
                v.memset(token[:, 4 + L:5 + L], 0.0).then_inc(u_free, USLOTS)

                for b in range(BLOCKS):
                    v.scalar_tensor_tensor(xn[:, b, :], h[:, b, :], rstd[:, b:b + 1], gB[:, :],
                                           ALU.mult, ALU.mult).then_inc(xn_ready, 1)
                    dve.wait_ge(xn_ready, BLOCKS * L + b + 1)
                    heads = (L * BLOCKS + b) * HEADS
                    with dve.Fori(0, HEADS) as i:
                        n = [0]

                        def routed(ins, unfused=False):
                            n[0] += 1
                            ins.then_inc(route_step, 1)
                            value = i * ROUTE_STEPS + (heads * ROUTE_STEPS + n[0])
                            if unfused:
                                wait_unfused(dve, (route_step, value))
                            else:
                                dve.wait_ge(route_step, value)

                        def top16(values, spare, best_, besti_):
                            routed(v.max(best_[0], values), True)
                            routed(v.max_index(besti_[0], best_[0], values), True)
                            routed(v.match_replace(spare, best_[0], values, LOWEST), True)
                            routed(v.max(best_[1], spare), True)
                            routed(v.max_index(besti_[1], best_[1], spare), True)

                        wait_unfused(dve, (head_in, i + (heads + 1)))
                        for p2 in range(2):
                            halves = [slice(0, 8), slice(8, 16)]
                            top16(sc[:, p2, :], sc2[:, p2, :], [top[:, p2, x] for x in halves],
                                  [topi[:, p2, x] for x in halves])
                        routed(v.tensor_scalar(topf[:, 0, :], topi[:, 0, :], float(NKEYS * L), None, ALU.add))
                        routed(v.tensor_copy(topf[:, 1, :], topi[:, 1, :]))
                        routed(v.tensor_tensor(cand[:, :, :], top[:, 0, :, None].to_broadcast([P, TOPK, TOPK]),
                                               top[:, 1, None, :].to_broadcast([P, TOPK, TOPK]), ALU.add), True)
                        flat = cand[:, :, :].rearrange("p a b -> p (a b)")
                        top16(flat, cand2[:, :], [best[:, x] for x in halves], [besti[:, x] for x in halves])
                        v.tensor_scalar(below[:, :], best[:, :], best[:, 0:1], None, ALU.subtract)\
                            .then_inc(under_max, 1)
                        routed(v.tensor_scalar(pos[:, 0, :], besti[:, :], 4, None, ALU.logical_shift_right))
                        routed(v.tensor_scalar(pos[:, 1, :], besti[:, :], TOPK - 1, None, ALU.bitwise_and))
                        for p2 in range(2):
                            o = onehot[:, p2, :, :]
                            routed(v.tensor_tensor(o, pos[:, p2, :, None].to_broadcast([P, TOPK, TOPK]),
                                                   iota16[:, None, :].to_broadcast([P, TOPK, TOPK]), ALU.is_equal))
                            routed(v.tensor_tensor(o, o, topf[:, p2, None, :].to_broadcast([P, TOPK, TOPK]),
                                                   ALU.mult))
                            routed(v.tensor_reduce(key[:, p2, :], o, AX.X, ALU.add))
                        v.scalar_tensor_tensor(expert_u[:, :], key[:, 0, :], float(NKEYS), key[:, 1, :],
                                               ALU.mult, ALU.add).then_inc(experts_u, 1)
                        for j in range(TOPK):
                            slot = uslot[j % USLOTS]
                            per = TOPK // USLOTS
                            dve.wait_ge(u_in[j % USLOTS],
                                        i * (16 * per) + 16 * (heads * per + j // USLOTS + 1))
                            v.tensor_tensor_reduce(out=slot, in0=slot, in1=xn[:, b, :], scale=1.0, scalar=0.0,
                                                   op0=ALU.mult, op1=ALU.add,
                                                   accum_out=dots[:, j:j + 1]).then_inc(u_free, 1)
                            if j == TOPK // 2 - 1:
                                dve.wait_ge(exp_done, i + (heads + 1))
                                routed(v.reciprocal(denom[:, 1:2], denom[:, 0:1]))
                                v.tensor_scalar(gates[:, :], expo[:, :], denom[:, 1:2], None, ALU.mult)\
                                    .then_inc(route_step, 1)
                                n[0] += 1
                                dve.wait_ge(v_free, i * TOPK + (L * SLOTS_FREED_V + VSLOTS + b * HEADS * TOPK))
                                v.scalar_tensor_tensor(expert_v[:, :], key[:, 0, :], float(NKEYS), key[:, 1, :],
                                                       ALU.mult, ALU.add).then_inc(experts_v, 1)
                        assert n[0] == ROUTE_STEPS, n
                        dve.wait_ge(gelu_done, i + (heads + 1))
                        dve.wait_ge(route_step, i * ROUTE_STEPS + (heads + 1) * ROUTE_STEPS)
                        v.tensor_tensor(weight[:, :], gelu[:, :], gates[:, :], ALU.mult).then_inc(weights_done, 1)

                b, rows = BLOCKS - 1, ((L + 1) * BLOCKS * HEADS - 1) * TOPK
                dve.wait_ge(weights_done, (L + 1) * BLOCKS * HEADS)
                dve.wait_ge(v_free, (L + 1) * SLOTS_FREED_V - 2 * TOPK)
                for n, j in enumerate(DVE_ROWS):
                    dve.wait_ge(v_in[j % VSLOTS], 16 * (rows // VSLOTS + j // VSLOTS + 1))
                    if n == 0:
                        row = v.tensor_scalar(h[:, b, :], vslot[j % VSLOTS], weight[:, j:j + 1], None, ALU.mult)
                    else:
                        row = v.scalar_tensor_tensor(h[:, b, :], vslot[j % VSLOTS], weight[:, j:j + 1], h[:, b, :],
                                                     ALU.mult, ALU.add)
                    row.then_inc(v_summed, 1)
                    dve.wait_ge(v_summed, L * len(DVE_ROWS) + n + 1)
                dve.wait_ge(block_done, (L + 1) * BLOCKS)
                v.tensor_tensor(h[:, b, :], ps[:, 4 * b:4 * b + 4, :].rearrange("p a n -> p (a n)"), h[:, b, :],
                                ALU.add).then_inc(h_expert, 1)

            dve.wait_ge(gain_in, 16 * (LAYERS + 1))
            for b in range(BLOCKS):
                norm_scale(2 * LAYERS, b)
                for half in range(2):
                    s = slice(half * D // 2, (half + 1) * D // 2)
                    v.scalar_tensor_tensor(xn[:, b, s], h[:, b, s], rstd[:, b:b + 1], gB[:, s],
                                           ALU.mult, ALU.mult).then_inc(result_ready, 1)


ROUTE_STEPS = 28

_INS = ['x', 'mix_norm_g', 'ffn_norm_g', 'ev_w_in', 'ev_pool_w', 'ev_pool_scale', 'ev_conv_w', 'ev_w_out',
        'od_w_in', 'od_v_norm_g', 'od_v_norm_b', 'od_sgu_w', 'od_sgu_b', 'od_conv_w', 'od_conv_b',
        'od_gn_g', 'od_gn_b', 'od_w_out', 'peer_w_q', 'peer_subkeys', 'peer_u', 'peer_v', 'final_norm_g']


def kernel(**inputs):
    import numpy as np
    import concourse.bacc as bacc
    from concourse import mybir as mb
    from concourse.bass_utils import run_bass_kernel_spmd as run

    nc = bacc.Bacc("TRN2", target_bir_lowering=False, num_devices=1)
    arrays, args = {}, []
    for name in _INS:
        a = np.ascontiguousarray(inputs[name])
        arrays[f"in_{name}"] = a
        args.append(nc.dram_tensor(f"in_{name}", a.shape, mb.dt.from_np(a.dtype), kind="ExternalInput").ap())
    args.append(nc.dram_tensor("out", (1, SEQ, D), mb.dt.float32, kind="ExternalOutput").ap())
    two_layers(nc, *args)
    return run(nc, [arrays], core_ids=[0]).results[0]["out"]
```
